# Optimizing a Trainium2 kernel written in Bass

```python
import math
import jax, jax.numpy as jnp
from jax import lax
import numpy as np

D_MODEL = 2048
BATCH = 1
SEQ = 256
DEPTH = 1
DEC_BATCH = 8
DEC_SEQ = 4
PAST_LEN = 2048
PAGE_SIZE = 128

BRANCH_W = D_MODEL // 2
N_BRANCH = 5
S5_GROUP = 16
S5_GROUPS = BRANCH_W // S5_GROUP
S5_STATE = 64
HG_HEADS = 8
HG_DK = BRANCH_W // HG_HEADS
HG_DV = BRANCH_W // HG_HEADS
GLA_HEADS = 4
GLA_KEY_W = BRANCH_W // 2
GLA_DK = GLA_KEY_W // GLA_HEADS
GLA_DV = BRANCH_W // GLA_HEADS
GLA_RANK = 16
GLA_GATE_TEMP = 16.0
LRU_BLOCKS = 8
LRU_BW = BRANCH_W // LRU_BLOCKS
CONV_W = 4
LRU_C = 8.0
N_MEM = 256
MEM_HEADS = 4
MEM_HD = BRANCH_W // MEM_HEADS

CHUNK = 64
EPS = 1e-6

IN_SPLITS = (
    ("a_x", BRANCH_W), ("a_g", BRANCH_W),
    ("b_q", BRANCH_W), ("b_f", BRANCH_W), ("b_i", BRANCH_W), ("b_g", BRANCH_W),
    ("c_q", GLA_KEY_W), ("c_k", GLA_KEY_W), ("c_v", BRANCH_W), ("c_r", GLA_RANK), ("c_g", BRANCH_W),
    ("d_x", BRANCH_W), ("d_g", BRANCH_W),
    ("e_q", BRANCH_W), ("e_g", BRANCH_W),
)
IN_WIDTH = sum(w for _, w in IN_SPLITS)

kernel_name = "hybrid_s5_hgrn2_gla_rglru_memxattn_step"

F32 = jnp.float32

def rmsnorm(x, g):
    xf = x.astype(F32)
    y = xf * lax.rsqrt(jnp.mean(xf * xf, axis=-1, keepdims=True) + EPS)
    return (y * g.astype(F32)).astype(x.dtype)

def split_cols(proj):
    out = {}
    off = 0
    for name, w in IN_SPLITS:
        out[name] = proj[..., off:off + w]
        off += w
    return out

def s5_branch(u, h0_re, h0_im, lam_re, lam_im, log_dt, b_re, b_im, c_re, c_im, d_skip, w_glu):
    n, t, _ = u.shape
    uf = u.astype(F32)
    ug = uf.reshape(n, t, S5_GROUPS, S5_GROUP)
    dt = jnp.exp(log_dt.astype(F32))[:, None]
    lr, li = lam_re.astype(F32), lam_im.astype(F32)
    mag = jnp.exp(lr * dt)
    ar, ai = mag * jnp.cos(li * dt), mag * jnp.sin(li * dt)
    den = lr * lr + li * li
    zr = ((ar - 1.0) * lr + ai * li) / den
    zi = (ai * lr - (ar - 1.0) * li) / den
    br, bi = b_re.astype(F32), b_im.astype(F32)
    bbr = zr[..., None] * br - zi[..., None] * bi
    bbi = zr[..., None] * bi + zi[..., None] * br
    xr = jnp.einsum("ntgh,gph->ntgp", ug, bbr)
    xi = jnp.einsum("ntgh,gph->ntgp", ug, bbi)
    h0r, h0i = h0_re.astype(F32), h0_im.astype(F32)
    xr = xr.at[:, 0].add(ar * h0r - ai * h0i)
    xi = xi.at[:, 0].add(ar * h0i + ai * h0r)
    are = jnp.broadcast_to(ar, xr.shape)
    aim = jnp.broadcast_to(ai, xi.shape)

    def combine(e1, e2):
        a1r, a1i, b1r, b1i = e1
        a2r, a2i, b2r, b2i = e2
        return (a2r * a1r - a2i * a1i, a2r * a1i + a2i * a1r,
                a2r * b1r - a2i * b1i + b2r, a2r * b1i + a2i * b1r + b2i)

    _, _, hr, hi = lax.associative_scan(combine, (are, aim, xr, xi), axis=1)
    y = jnp.einsum("gop,ntgp->ntgo", c_re.astype(F32), hr) - jnp.einsum("gop,ntgp->ntgo", c_im.astype(F32), hi)
    y = y.reshape(n, t, BRANCH_W) + d_skip.astype(F32) * uf
    z = jax.nn.gelu(y)
    out = z * jax.nn.sigmoid(z @ w_glu.astype(F32))
    return out, hr[:, -1], hi[:, -1]

def chunk_gla(q, k, v, log_f, s0):
    n, t, h, dk = q.shape
    dv = v.shape[-1]
    L = min(CHUNK, t)
    nc = -(-t // L)
    pad = nc * L - t
    if pad:
        pw = ((0, 0), (0, pad), (0, 0), (0, 0))
        q, k, v, log_f = [jnp.pad(a, pw) for a in (q, k, v, log_f)]

    def to_chunks(a):
        return a.reshape(n, nc, L, h, a.shape[-1]).transpose(1, 0, 3, 2, 4)

    qc, kc, vc, fc = [to_chunks(a) for a in (q, k, v, log_f)]
    mask = jnp.tril(jnp.ones((L, L), dtype=bool))[:, :, None]

    def step(S, inp):
        qi, ki, vi, gi = inp
        b = jnp.cumsum(gi, axis=2)
        inter = jnp.einsum("nhtk,nhkv->nhtv", qi * jnp.exp(b), S)
        diff = b[:, :, :, None, :] - b[:, :, None, :, :]
        decay = jnp.where(mask, jnp.exp(jnp.where(mask, diff, 0.0)), 0.0)
        att = jnp.einsum("nhtk,nhsk,nhtsk->nhts", qi, ki, decay)
        intra = jnp.einsum("nhts,nhsv->nhtv", att, vi)
        b_last = b[:, :, -1]
        S_new = jnp.exp(b_last)[..., None] * S + jnp.einsum(
            "nhsk,nhsv->nhkv", ki * jnp.exp(b_last[:, :, None] - b), vi)
        return S_new, inter + intra

    S, o = lax.scan(step, s0, (qc, kc, vc, fc))
    o = o.transpose(1, 0, 3, 2, 4).reshape(n, nc * L, h, dv)[:, :t]
    return o, S

def hgrn2_branch(q, fz, i, s0, lb, g_norm):
    n, t, _ = q.shape
    shp = (n, t, HG_HEADS, HG_DK)
    fz = fz.astype(F32)
    lb = lb.astype(F32)
    log_f = jnp.logaddexp(jnp.log(lb), jnp.log1p(-lb) + jax.nn.log_sigmoid(fz))
    k = (1.0 - lb) * jax.nn.sigmoid(-fz)
    o, s = chunk_gla(q.astype(F32).reshape(shp), k.reshape(shp),
                     i.astype(F32).reshape(n, t, HG_HEADS, HG_DV), log_f.reshape(shp), s0.astype(F32))
    o = rmsnorm(o, g_norm).reshape(n, t, BRANCH_W)
    return o, s

def gla_branch(q, k, v, r, s0, w_up, b_up, g_norm):
    n, t, _ = q.shape
    shp = (n, t, GLA_HEADS, GLA_DK)
    log_a = jax.nn.log_sigmoid(r.astype(F32) @ w_up.astype(F32) + b_up.astype(F32)) / GLA_GATE_TEMP
    qh = q.astype(F32).reshape(shp) * (GLA_DK ** -0.5)
    o, s = chunk_gla(qh, k.astype(F32).reshape(shp), v.astype(F32).reshape(n, t, GLA_HEADS, GLA_DV),
                     log_a.reshape(shp), s0.astype(F32))
    o = rmsnorm(o, g_norm).reshape(n, t, BRANCH_W)
    return o, s

def rglru_branch(xd, conv_buf, h0, conv_w, conv_b, w_r, b_r, w_i, b_i, lam):
    n, t, _ = xd.shape
    xcat = jnp.concatenate([conv_buf.astype(F32), xd.astype(F32)], axis=1)
    cw = conv_w.astype(F32)
    xc = conv_b.astype(F32) + sum(cw[j] * xcat[:, j:j + t] for j in range(CONV_W))
    new_buf = xcat[:, t:]
    xb = xc.reshape(n, t, LRU_BLOCKS, LRU_BW)
    r = jax.nn.sigmoid(jnp.einsum("ntbi,bio->ntbo", xb, w_r.astype(F32)).reshape(n, t, BRANCH_W) + b_r.astype(F32))
    ig = jax.nn.sigmoid(jnp.einsum("ntbi,bio->ntbo", xb, w_i.astype(F32)).reshape(n, t, BRANCH_W) + b_i.astype(F32))
    log_a = -LRU_C * r * jax.nn.softplus(-lam.astype(F32))
    a = jnp.exp(log_a)
    u = jnp.sqrt(-jnp.expm1(2.0 * log_a)) * (ig * xc)
    u = u.at[:, 0].add(a[:, 0] * h0.astype(F32))

    def combine(e1, e2):
        a1, b1 = e1
        a2, b2 = e2
        return a1 * a2, a2 * b1 + b2

    _, hseq = lax.associative_scan(combine, (a, u), axis=1)
    return hseq, hseq[:, -1], new_buf

def mem_attend(q, mk, mv):
    n, t, _ = q.shape
    qh = q.astype(F32).reshape(n, t, MEM_HEADS, MEM_HD) * (MEM_HD ** -0.5)
    s = jnp.einsum("nthd,nmhd->nhtm", qh, mk.astype(F32))
    pr = jax.nn.softmax(s, axis=-1)
    return jnp.einsum("nhtm,nmhd->nthd", pr, mv.astype(F32)).reshape(n, t, BRANCH_W)

def trunk(x, mem_k, mem_v, s5_re, s5_im, hg_s, gla_s, lru_h, conv_buf, hg_lb, weights):
    (norm_pre, norm_post, w_in, s5_lam_re, s5_lam_im, s5_log_dt, s5_b_re, s5_b_im, s5_c_re, s5_c_im,
     s5_d, s5_w_glu, hg_norm, gla_w_up, gla_b_up, gla_norm, conv_w, conv_b, lru_w_r, lru_b_r,
     lru_w_i, lru_b_i, lru_lam, w_branch, w_merge, w_out) = weights
    n, t, _ = x.shape
    outs = ([], [], [], [], [], [])
    for l in range(DEPTH):
        h = rmsnorm(x, norm_pre[l])
        p = split_cols(h @ w_in[l])
        oa, a_re, a_im = s5_branch(p["a_x"], s5_re[l], s5_im[l], s5_lam_re[l], s5_lam_im[l], s5_log_dt[l],
                                   s5_b_re[l], s5_b_im[l], s5_c_re[l], s5_c_im[l], s5_d[l], s5_w_glu[l])
        ob, hs = hgrn2_branch(p["b_q"], p["b_f"], p["b_i"], hg_s[l], hg_lb[l], hg_norm[l])
        oc, gs = gla_branch(p["c_q"], p["c_k"], p["c_v"], p["c_r"], gla_s[l], gla_w_up[l], gla_b_up[l], gla_norm[l])
        od, lh, cb = rglru_branch(p["d_x"], conv_buf[l], lru_h[l], conv_w[l], conv_b[l],
                                  lru_w_r[l], lru_b_r[l], lru_w_i[l], lru_b_i[l], lru_lam[l])
        oe = mem_attend(p["e_q"], mem_k[l], mem_v[l])
        silu = lambda g: jax.nn.silu(g.astype(F32))
        branches = jnp.stack([oa * silu(p["a_g"]), ob * silu(p["b_g"]), oc * silu(p["c_g"]),
                              od * silu(p["d_g"]), oe * silu(p["e_g"])], axis=2).astype(x.dtype)
        pb = jnp.einsum("ntcw,cwd->ntcd", branches, w_branch[l])
        gate = jax.nn.sigmoid(h @ w_merge[l]).reshape(n, t, N_BRANCH, D_MODEL)
        merged = jnp.einsum("ntcd,ntcd->ntd", gate, pb)
        x = x + rmsnorm(merged @ w_out[l], norm_post[l])
        for lst, val in zip(outs, (a_re, a_im, hs, gs, lh, cb)):
            lst.append(val.astype(x.dtype))
    return x, [jnp.stack(lst) for lst in outs]

def setup_inputs(seed: int = 0) -> dict:
    key = jax.random.key(seed)
    counter = [0]

    def nxt():
        counter[0] += 1
        return jax.random.fold_in(key, counter[0])

    def nrm(shape, scale):
        return scale * jax.random.normal(nxt(), shape, F32)

    def gain(shape):
        return 1.0 + nrm(shape, 0.05)

    W = BRANCH_W
    d = {}
    d["x_prompt"] = nrm((BATCH, SEQ, D_MODEL), 1.0)
    d["x_sample"] = nrm((DEC_BATCH, DEC_SEQ, D_MODEL), 1.0)
    d["mem_prompt"] = nrm((BATCH, N_MEM, D_MODEL), 1.0)
    d["state_s5_re"] = nrm((DEPTH, DEC_BATCH, S5_GROUPS, S5_STATE), 0.5)
    d["state_s5_im"] = nrm((DEPTH, DEC_BATCH, S5_GROUPS, S5_STATE), 0.5)
    d["state_hgrn"] = nrm((DEPTH, DEC_BATCH, HG_HEADS, HG_DK, HG_DV), 0.3)
    d["state_gla"] = nrm((DEPTH, DEC_BATCH, GLA_HEADS, GLA_DK, GLA_DV), 0.3)
    d["state_rglru"] = nrm((DEPTH, DEC_BATCH, W), 0.5)
    d["state_conv"] = nrm((DEPTH, DEC_BATCH, CONV_W - 1, W), 1.0)
    d["cache_mem_k"] = nrm((DEPTH, DEC_BATCH, N_MEM, MEM_HEADS, MEM_HD), 1.0)
    d["cache_mem_v"] = nrm((DEPTH, DEC_BATCH, N_MEM, MEM_HEADS, MEM_HD), 1.0)
    d["norm_pre"] = gain((DEPTH, D_MODEL))
    d["norm_post"] = gain((DEPTH, D_MODEL))
    d["w_in"] = nrm((DEPTH, D_MODEL, IN_WIDTH), D_MODEL ** -0.5)
    d["s5_lam_re"] = -0.5 * jnp.exp(nrm((DEPTH, S5_GROUPS, S5_STATE), 0.05))
    d["s5_lam_im"] = jnp.pi * jnp.arange(S5_STATE, dtype=F32) + nrm((DEPTH, S5_GROUPS, S5_STATE), 0.01)
    d["s5_log_dt"] = jax.random.uniform(nxt(), (DEPTH, S5_GROUPS), F32, math.log(1e-3), math.log(1e-1))
    d["s5_b_re"] = nrm((DEPTH, S5_GROUPS, S5_STATE, S5_GROUP), (2.0 * S5_GROUP) ** -0.5)
    d["s5_b_im"] = nrm((DEPTH, S5_GROUPS, S5_STATE, S5_GROUP), (2.0 * S5_GROUP) ** -0.5)
    d["s5_c_re"] = nrm((DEPTH, S5_GROUPS, S5_GROUP, S5_STATE), (2.0 * S5_STATE) ** -0.5)
    d["s5_c_im"] = nrm((DEPTH, S5_GROUPS, S5_GROUP, S5_STATE), (2.0 * S5_STATE) ** -0.5)
    d["s5_d"] = nrm((DEPTH, W), 1.0)
    d["s5_w_glu"] = nrm((DEPTH, W, W), W ** -0.5)
    d["hg_lb_logits"] = nrm((DEPTH, W), 0.1)
    d["hg_norm"] = gain((DEPTH, HG_DV))
    d["gla_w_up"] = nrm((DEPTH, GLA_RANK, GLA_KEY_W), GLA_RANK ** -0.5)
    d["gla_b_up"] = nrm((DEPTH, GLA_KEY_W), 0.1)
    d["gla_norm"] = gain((DEPTH, GLA_DV))
    d["conv_w"] = nrm((DEPTH, CONV_W, W), CONV_W ** -0.5)
    d["conv_b"] = nrm((DEPTH, W), 0.01)
    d["lru_w_r"] = nrm((DEPTH, LRU_BLOCKS, LRU_BW, LRU_BW), LRU_BW ** -0.5)
    d["lru_b_r"] = nrm((DEPTH, W), 0.01)
    d["lru_w_i"] = nrm((DEPTH, LRU_BLOCKS, LRU_BW, LRU_BW), LRU_BW ** -0.5)
    d["lru_b_i"] = nrm((DEPTH, W), 0.01)
    a0 = jax.random.uniform(nxt(), (DEPTH, W), F32, 0.9, 0.999)
    s = a0 ** (1.0 / LRU_C)
    d["lru_lam"] = jnp.log(s) - jnp.log1p(-s)
    d["mem_norm"] = gain((DEPTH, D_MODEL))
    d["w_mem_k"] = nrm((DEPTH, D_MODEL, W), D_MODEL ** -0.5)
    d["w_mem_v"] = nrm((DEPTH, D_MODEL, W), D_MODEL ** -0.5)
    d["w_branch"] = nrm((DEPTH, N_BRANCH, W, D_MODEL), W ** -0.5)
    d["w_merge"] = nrm((DEPTH, D_MODEL, N_BRANCH * D_MODEL), D_MODEL ** -0.5)
    d["w_out"] = nrm((DEPTH, D_MODEL, D_MODEL), D_MODEL ** -0.5)
    return d

def reference(x_prompt, x_sample, mem_prompt, state_s5_re, state_s5_im, state_hgrn, state_gla, state_rglru,
              state_conv, cache_mem_k, cache_mem_v, norm_pre, norm_post, w_in, s5_lam_re, s5_lam_im, s5_log_dt,
              s5_b_re, s5_b_im, s5_c_re, s5_c_im, s5_d, s5_w_glu, hg_lb_logits, hg_norm, gla_w_up, gla_b_up,
              gla_norm, conv_w, conv_b, lru_w_r, lru_b_r, lru_w_i, lru_b_i, lru_lam, mem_norm, w_mem_k, w_mem_v,
              w_branch, w_merge, w_out):
    weights = (norm_pre, norm_post, w_in, s5_lam_re, s5_lam_im, s5_log_dt, s5_b_re, s5_b_im, s5_c_re, s5_c_im,
               s5_d, s5_w_glu, hg_norm, gla_w_up, gla_b_up, gla_norm, conv_w, conv_b, lru_w_r, lru_b_r,
               lru_w_i, lru_b_i, lru_lam, w_branch, w_merge, w_out)
    lb = jnp.cumsum(jax.nn.softmax(hg_lb_logits.astype(F32), axis=0), axis=0)
    hg_lb = lb - lb[:1]

    nb = x_prompt.shape[0]
    mk, mv = [], []
    for l in range(DEPTH):
        m = rmsnorm(mem_prompt, mem_norm[l])
        mk.append((m @ w_mem_k[l]).reshape(nb, N_MEM, MEM_HEADS, MEM_HD))
        mv.append((m @ w_mem_v[l]).reshape(nb, N_MEM, MEM_HEADS, MEM_HD))
    p_mem_k = jnp.stack(mk)
    p_mem_v = jnp.stack(mv)
    dt = x_prompt.dtype
    z_s5 = jnp.zeros((DEPTH, nb, S5_GROUPS, S5_STATE), dt)
    z_hg = jnp.zeros((DEPTH, nb, HG_HEADS, HG_DK, HG_DV), dt)
    z_gla = jnp.zeros((DEPTH, nb, GLA_HEADS, GLA_DK, GLA_DV), dt)
    z_lru = jnp.zeros((DEPTH, nb, BRANCH_W), dt)
    z_conv = jnp.zeros((DEPTH, nb, CONV_W - 1, BRANCH_W), dt)
    y_prompt, (p_s5_re, p_s5_im, p_hgrn, p_gla, p_rglru, p_conv) = trunk(
        x_prompt, p_mem_k, p_mem_v, z_s5, z_s5, z_hg, z_gla, z_lru, z_conv, hg_lb, weights)

    y_sample, (s_s5_re, s_s5_im, s_hgrn, s_gla, s_rglru, s_conv) = trunk(
        x_sample, cache_mem_k, cache_mem_v, state_s5_re, state_s5_im, state_hgrn, state_gla,
        state_rglru, state_conv, hg_lb, weights)

    return (y_prompt, y_sample, p_s5_re, p_s5_im, p_hgrn, p_gla, p_rglru, p_conv, p_mem_k, p_mem_v,
            s_s5_re, s_s5_im, s_hgrn, s_gla, s_rglru, s_conv)


_drawn_inputs = setup_inputs


def setup_inputs(seed=0):
    import zlib

    import numpy as np

    out = dict(_drawn_inputs(seed))
    spreads = {}
    factors = {'lru_b_r': 26.042, 'lru_b_i': 8.0}
    for name, (base, spread) in spreads.items():
        noise = np.random.default_rng([zlib.crc32(name.encode()), seed]).standard_normal(out[name].shape)
        drawn = base * np.exp(spread * noise) if base else spread * noise
        out[name] = __import__('jax').numpy.asarray(drawn.astype(out[name].dtype))
    for name, factor in factors.items():
        out[name] = (out[name] * factor).astype(out[name].dtype)
    return out
```

```python
from contextlib import ExitStack

import numpy as np
import concourse.bass as bass
from concourse import mybir

F32 = mybir.dt.float32
F32R = mybir.dt.float32r
ACT = mybir.ActivationFunctionType
ALU = mybir.AluOpType
AX = mybir.AxisListType

P = 128
D_MODEL = 2048
SEQ, NB, NT = 256, 8, 4
TS = NB * NT
T = SEQ + TS
KT = D_MODEL // P
W = D_MODEL // 2
WT = W // P
N_MEM = 256
HD = 256
EPS = 1e-6
CHUNK = 64
LRU_C = 8.0
GLA_RANK = 16
UK = 8
SLOTS = 4
N_SEQ = 1 + NB

STAGES = [("E", 4, 16, 8), ("mE", 4, 12, 8), ("D", 8, 4, 2), ("mD", 4, 12, 8), ("C", 4, 12, 6),
          ("mC", 4, 12, 8), ("B", 8, 8, 4), ("mB", 4, 12, 8), ("A", 8, 4, 2), ("glu", 2, 4, 4),
          ("mA", 4, 12, 8), ("out", 8, 4, 2)]
UNIT0, BLOCK0, UNITS = {}, {}, {}
_u = _b = 0
for _name, _n, _nu, _nb in STAGES:
    UNIT0[_name], BLOCK0[_name], UNITS[_name] = _u, _b, _nu
    _u += _n * _nu
    _b += _n * _nb
N_UNITS = _u
N_BLOCKS = {name: nb for name, _, _, nb in STAGES}
HALVES = [64, 32, 16, 8, 4, 2, 1]
LINKS = {"E": 5, "D": 19, "C": 14, "B": 13, "A": 46}
ROUND = 12582912.0
TWO_PI = (6.28125, 0.0019350051879882812, 3.0199159819567e-07)
PI_IN = 3.1415925
DIAG, CROSS, FINAL = 7, 7, 8


class Chain:

    def __init__(self, eng, sem):
        self.eng, self.sem, self.base, self.k, self.i, self.per = eng, sem, 0, 0, None, 0

    def enter(self, i, per):
        self.base, self.k, self.i, self.per = self.base + self.k, 0, i, per

    def leave(self, n):
        assert self.k == self.per, f"a body has {self.k} links, {self.per} said"
        self.base, self.k, self.i = self.base + n * self.per, 0, None

    def link(self, ins):
        ins.then_inc(self.sem, 1)
        self.k += 1
        at = self.base + self.k
        self.eng.wait_ge(self.sem, at if self.i is None else self.i * self.per + at)


def build(nc, t):
    ctx = ExitStack()
    with ctx:
        def sb(name, shape, dt=F32, stack=ctx):
            return stack.enter_context(nc.sbuf_tensor(name, shape, dt))

        sems = {}

        def S(name):
            if name not in sems:
                sems[name] = ctx.enter_context(nc.semaphore(name))
            return sems[name]

        raw = sb("raw", [P, SLOTS, UK, P])
        w_hi = sb("w_hi", [P, SLOTS, UK, P], F32R)
        w_lo = sb("w_lo", [P, SLOTS, UK, P], F32R)
        h_hi = sb("h_hi", [P, KT, T], F32R)
        h_lo = sb("h_lo", [P, KT, T], F32R)
        br_hi = sb("br_hi", [P, WT, T], F32R)
        br_lo = sb("br_lo", [P, WT, T], F32R)
        acc = sb("acc", [P, KT, T])
        ident = sb("ident", [P, P])
        ones = sb("ones", [P, P])
        levels = sb("levels", [P, 8, P])
        starts = sb("starts", [P, T])
        chunks = sb("chunks", [P, T])
        in_group = sb("in_group", [P, 8])
        st_group = sb("st_group", [P, 4, 8])
        in_seq = sb("in_seq", [TS, NB])
        norm_cols = sb("norm_cols", [P, 3, KT])
        zero = sb("zero", [P, 1])
        eps = sb("eps", [P, 1])
        half_pi = sb("half_pi", [P, 1])
        rstd = sb("rstd", [P, T])
        sd = sb("sd", [P, T])
        half_out = sb("half_out", [P, T])
        gate_t = sb("gate_t", [P, T])

        e_st = ExitStack()
        m_hi = sb("m_hi", [P, KT, N_MEM], F32R, e_st)
        m_lo = sb("m_lo", [P, KT, N_MEM], F32R, e_st)
        vc = sb("vc", [P, 2, NB, HD], F32, e_st)
        eq = sb("eq", [P, 2, T], F32, e_st)
        e_gate = sb("e_gate", [P, 2, T], F32, e_st)
        e_th = sb("e_th", [P, 2, T], F32, e_st)
        kT = sb("kT", [P, 2, N_MEM], F32, e_st)
        vT = sb("vT", [P, 2, N_MEM], F32, e_st)
        vm = sb("vm", [P, 2, HD], F32, e_st)
        ssc = sb("ssc", [P, 2, TS], F32, e_st)
        prob = sb("prob", [P, 3, N_MEM], F32, e_st)
        mx = sb("mx", [P, 3], F32, e_st)
        rs = sb("rs", [P, 3], F32, e_st)
        pT = sb("pT", [P, 2, T], F32, e_st)
        e_out = sb("e_out", [P, 2, T], F32, e_st)
        e_st.close()
        kc = acc[:].rearrange("p k t -> p (k t)")[:, 0:2 * NB * N_MEM].rearrange(
            "p (d b m) -> p d b m", d=2, b=NB)

        n_st = ExitStack()
        sb("n_pad", [P, 2 * KT * N_MEM], F32R, n_st)
        sq = sb("sq", [P, KT * T], F32, n_st)
        n_st.close()
        o_st = ExitStack()
        x_res = sb("x_res", [P, KT, T], F32, o_st)
        o_sq = sb("o_sq", [P, KT * T], F32, o_st)
        o_st.close()

        d_st = ExitStack()
        d_cols = sb("d_cols", [P, 8, WT], F32, d_st)
        d_sp = sb("d_sp", [P, 8, WT], F32, d_st)
        d_cbuf = sb("d_cbuf", [P, WT, NB, 3], F32, d_st)
        d_h0 = sb("d_h0", [P, WT, NB], F32, d_st)
        d_w = sb("d_w", [P, 2, P], F32, d_st)
        d_xp = sb("d_xp", [P, SEQ + 3], F32, d_st)
        d_xs = sb("d_xs", [P, NB, NT + 3], F32, d_st)
        xc = sb("xc", [P, T], F32, d_st)
        d_r = sb("d_r", [P, T], F32, d_st)
        d_i = sb("d_i", [P, T], F32, d_st)
        d_a = sb("d_a", [P, T], F32, d_st)
        d_L = sb("d_L", [P, T], F32, d_st)
        d_t = sb("d_t", [P, T], F32, d_st)
        d_u = sb("d_u", [P, T], F32, d_st)
        d_gate = sb("d_gate", [P, T], F32, d_st)
        d_th = sb("d_th", [P, T], F32, d_st)
        d_hseq = sb("d_hseq", [P, T], F32, d_st)
        d_out = sb("d_out", [P, T], F32, d_st)
        d_inj = sb("d_inj", [P, NB], F32, d_st)
        d_hlast = sb("d_hlast", [P, WT, N_SEQ], F32, d_st)
        d_clast = sb("d_clast", [P, WT, N_SEQ, 3], F32, d_st)
        d_st.close()

        g_st = ExitStack()
        g_S0 = sb("g_S0", [P, NB, 256], F32, g_st)
        g_X = sb("g_X", [P, 9, T], F32, g_st)
        g_prod = sb("g_prod", [P, 8, P], F32, g_st)
        g_att = sb("g_att", [P, 3, P], F32, g_st)
        g_atts = sb("g_atts", [TS, TS], F32, g_st)
        g_q = sb("g_q", [P, T], F32, g_st)
        g_k = sb("g_k", [P, T], F32, g_st)
        g_g = sb("g_g", [P, T], F32, g_st)
        g_b = sb("g_b", [P, T], F32, g_st)
        g_v = sb("g_v", [P, 2, T], F32, g_st)
        g_vT = sb("g_vT", [P, 3, 256], F32, g_st)
        g_kT = sb("g_kT", [P, 3, P], F32, g_st)
        g_vm = sb("g_vm", [TS, 1024], F32, g_st)
        g_gs = sb("g_gs", [P, 2, T], F32, g_st)
        g_t = sb("g_t", [P, 4, T], F32, g_st)
        g_o2 = sb("g_o2", [P, 2, T], F32, g_st)
        g_Sp = sb("g_Sp", [P, 256], F32, g_st)
        g_eb = sb("g_eb", [P, NB], F32, g_st)
        g_bb = sb("g_bb", [P, 1], F32, g_st)
        g_e = sb("g_e", [P, 2, T], F32, g_st)
        g_o = sb("g_o", [P, 2, T], F32, g_st)
        g_cols = sb("g_cols", [P, 8], F32, g_st)
        g_lb = sb("g_lb", [P, 4, WT], F32, g_st)
        g_wr = sb("g_wr", [P, KT, GLA_RANK], F32, g_st)
        g_r = sb("g_r", [GLA_RANK, T], F32, g_st)
        g_wu = sb("g_wu", [GLA_RANK, P], F32, g_st)
        g_st.close()

        a_st = ExitStack()
        a_p = sb("a_p", [P, 2, 32, 16], F32, a_st)
        a_q = sb("a_q", [P, 2, 32, 16], F32, a_st)
        a_bb = sb("a_bb", [P, 2, WT, 64], F32, a_st)
        a_last = sb("a_last", [P, 2, 32, N_SEQ], F32, a_st)
        a_mag = sb("a_mag", [P, 32], F32, a_st)
        a_inj = a_last[:, :, :, 1:N_SEQ]
        a_d = sb("a_d", [P, WT], F32, a_st)
        a_c = sb("a_c", [P, 2, 32, 16], F32, a_st)
        a_cs = sb("a_cs", [P, 2, 32], F32, a_st)
        a_set_up = ExitStack()
        st_in = sb("st_in", [P, 3, 32], F32, a_set_up)
        ch_in = sb("ch_in", [P, 2, WT, 64], F32, a_set_up)
        ch_dt = sb("ch_dt", [P, WT], F32, a_set_up)[:]
        br_in = sb("br_in", [P, WT, 64], F32, a_set_up)
        bi_in = sb("bi_in", [P, WT, 64], F32, a_set_up)
        h0_in = sb("h0_in", [P, 2, 32, NB], F32, a_set_up)
        st_a, st_th, st_n, st_abs = (sb(f"st_{n}", [P, 32], F32, a_set_up)[:] for n in ("a", "th", "n", "abs"))
        st_tmp = sb("st_tmp", [P, 32, NB], F32, a_set_up)[:]
        ch_a, ch_th, ch_n, ch_mag, ch_sin, ch_cos, ch_abs = (
            sb(f"ch_{n}", [P, WT, 64], F32, a_set_up)[:] for n in ("a", "th", "n", "mag", "sin", "cos", "abs"))
        tab_t1 = sb("tab_t1", [P, 2, 32, 8], F32, a_set_up)
        tab_t2 = sb("tab_t2", [P, 2, 32, 8], F32, a_set_up)
        a_set_up.close()
        st_dt = st_in[:, 2]
        z_hi = sb("z_hi", [P, WT, T], F32R, a_st)
        z_lo = sb("z_lo", [P, WT, T], F32R, a_st)
        zg = sb("zg", [P, WT, T], F32, a_st)
        a_P = sb("a_P", [P, 2, 2, T], F32, a_st)
        a_t1 = sb("a_t1", [P, 2, 2, T], F32, a_st)
        a_t2 = sb("a_t2", [P, 2, 2, T], F32, a_st)
        a_m = sb("a_m", [P, 2, 2, T], F32, a_st)
        a_g = sb("a_g", [P, 2, 2, T], F32, a_st)
        a_r = sb("a_r", [P, 2, T], F32, a_st)
        a_B = sb("a_B", [P, 2, 8, 64], F32, a_st)
        a_C = levels[:].rearrange("p (k j) s -> p k j s", k=2)
        a_y, a_ud, a_gs, a_gate, a_th = rstd, half_out, sd, chunks, gate_t
        a_st.close()

        ps = ctx.enter_context(nc.psum_tensor("ps", [P, 8, 512], F32))
        up = ps[:, 5:7].rearrange("p a c -> p (a c)")

        landed = [S(f"landed{s}") for s in range(SLOTS)]
        hi_ready, lo_ready, slots_freed = S("hi_ready"), S("lo_ready"), S("slots_freed")
        bank_free = [S("bank_free0"), S("bank_free1")]
        merge_done = S("merge_done")

        def at(stage, i, u):
            return i * UNITS[stage] + (UNIT0[stage] + u)

        def earlier(stage, i, b):
            return i * (N_BLOCKS[stage] // 2) + (BLOCK0[stage] + b) // 2

        def wait_block(eng, stage, i, b, last_unit):
            eng.wait_ge(slots_freed, at(stage, i, last_unit) + (1 + SLOTS))

        def wait_taken(eng, stage, i, b):
            eng.wait_ge(bank_free[b % 2], earlier(stage, i, b) + 1)

        def by_seq(ap):
            return ap[:, SEQ:T].rearrange("p (b t) -> p b t", t=NT)

        def heads_before(i, nv):
            return (i, i * 2) if nv == 2 else (i + 4, i + 8)

        block = ctx.enter_context(nc.Block())

        @block.sync
        def _(sp):
            sp.dma_start(acc[:, :, 0:N_MEM], t["mem"]).then_inc(S("mem_landed"), 16)

            def load(unit, slot):
                sp.dma_start(raw[:, slot], t["w"][unit].rearrange("p (k c) -> p k c", k=UK)).then_inc(landed[slot], 16)

            for s in range(SLOTS):
                load(s, s)
            sp.wait_ge(S("m_split"), 1)
            sp.dma_start(acc[:], t["x"]).then_inc(S("x_landed"), 16)
            with sp.Fori(1, N_UNITS // SLOTS) as i:
                for s in range(SLOTS):
                    sp.wait_ge(lo_ready, i * SLOTS + (s - SLOTS + 1))
                    load(i * SLOTS + s, s)

        @block.gpsimd
        def _(pool):
            link = Chain(pool, S("pool_steps")).link

            def load(dst, src, name):
                pool.dma_start(dst, src).then_inc(S(name), 16)

            def wait_before_load(sem, count):
                pool.wait_ge(slots_freed, 1)
                pool.wait_ge(S(sem), count)

            pool.memset(zero[:], 0.0).then_inc(slots_freed, SLOTS)
            load(norm_cols[:], t["norms"], "norms_landed")
            link(pool.memset(ones[:], 1.0))
            link(pool.memset(eps[:], EPS))
            link(pool.memset(half_pi[:], float(np.pi / 2)))
            pool.memset(ident[:], 0.0).then_inc(S("ones_ready"), 1)
            pool.wait_ge(S("ones_ready"), 1)
            link(pool.affine_select(out=ident[:], in_=ident[:], compare_op=ALU.not_equal, fill=1.0,
                                    base=0, pattern=[[-1, P]], channel_multiplier=1))
            for mask, every in ((starts, SEQ), (chunks, CHUNK)):
                link(pool.memset(mask[:], 1.0))
                link(pool.memset(mask[:, 0:SEQ].rearrange("p (c t) -> p c t", t=every)[:, :, 0:1], 0.0))
                link(pool.memset(by_seq(mask)[:, :, 0:1], 0.0))
            link(pool.memset(levels[:], 0.0))
            for l, h in enumerate(HALVES):
                n = P // (2 * h)
                right = levels[:, l, :].rearrange("p (b two h) -> p b two h", two=2, h=h)[:, :, 1, :]
                link(pool.memset(right, 1.0))
                for base, sign in ((0, 1), (h - 1, -1)):
                    link(pool.affine_select(out=right, in_=right, compare_op=ALU.is_ge, fill=0.0, base=base,
                                            pattern=[[-2 * h * sign, n], [0, h]], channel_multiplier=sign))
            link(pool.affine_select(out=levels[:, DIAG, :], in_=levels[:, DIAG, :], compare_op=ALU.not_equal,
                                    fill=1.0, base=0, pattern=[[-1, P]], channel_multiplier=1))
            for mask, width, pattern in ((in_group[:], 16, [[-16, 8]]), (st_group[:], 64, [[128, 4], [-64, 8]]),
                                         (in_seq[:], NT, [[-NT, NB]])):
                link(pool.memset(mask, 1.0))
                for base, sign in ((0, 1), (width - 1, -1)):
                    link(pool.affine_select(out=mask, in_=mask, compare_op=ALU.is_ge, fill=0.0, base=base,
                                            pattern=[[a * sign, b] for a, b in pattern], channel_multiplier=sign))
            pool.memset(zero[:], 0.0).then_inc(S("masks_ready"), 1)

            pool.wait_ge(S("h_split"), 1)
            with pool.Fori(0, 4) as i:
                wait_before_load("e_scores", i * 3)
                load(kc, t["kc"][i], "kc_landed")
                wait_before_load("e_o", i)
                load(vc[:], t["vc"][i], "vc_landed")
                wait_before_load("bank_free0", earlier("E", i, 2) + 1)
                wait_before_load("bank_free1", earlier("E", i, 3) + 1)
                load(t["out_mem_k"][i], kT[:], "kv_stored")
                load(t["out_mem_v"][i], vT[:], "kv_stored")
            pool.wait_ge(S("kv_stored"), 32 * 4)

            pool.wait_ge(merge_done, 16)
            pool.memset(d_xp[:, 0:3], 0.0).then_inc(S("d_pad"), 1)
            load(d_cols[:], t["d_cols"], "d_params")
            load(d_cbuf[:], t["d_cbuf"], "d_params")
            load(d_h0[:], t["d_h0"], "d_params")
            with pool.Fori(0, WT) as i:
                wait_before_load("d_gates", i)
                load(d_w[:], t["d_w"][i], "d_w_landed")
            pool.wait_ge(S("d_lo"), WT)
            load(t["out_lru"], d_hlast[:], "d_stored")
            load(t["out_conv"], d_clast[:], "d_stored")
            pool.wait_ge(S("d_stored"), 32)

            pool.wait_ge(merge_done, 32)
            load(g_cols[:], t["g_cols"], "g_params")
            load(g_lb[:, 0], t["lb"], "g_params")
            load(g_wr[:], t["w_r"], "g_params")
            with pool.Fori(1, 5) as n:
                i = n - 1
                wait_before_load("c_z", i)
                load(g_wu[:], t["w_up"][i], "c_wu_landed")
                wait_before_load("g_stored", i * 32)
                load(g_S0[:], t["gla"][i], "g_S0_landed")
                wait_before_load("g_new", n)
                load(t["out_gla_s"][i], g_S0[:], "g_stored")
                wait_before_load("g_Sp", n)
                load(t["out_gla_p"][i], g_Sp[:], "g_stored")
            pool.wait_ge(S("g_stored"), 4 * 32)

            pool.wait_ge(merge_done, 48)
            with pool.Fori(5, 13) as n:
                i = n - 5
                wait_before_load("g_stored", i * 32 + 4 * 32)
                load(g_S0[:, :, 0:P], t["hgrn"][i], "g_S0_landed")
                wait_before_load("g_new", n)
                load(t["out_hg_s"][i], g_S0[:, :, 0:P], "g_stored")
                wait_before_load("g_Sp", n)
                load(t["out_hg_p"][i], g_Sp[:, 0:P], "g_stored")
            pool.wait_ge(S("g_stored"), 12 * 32)

            pool.wait_ge(merge_done, 64)
            load(st_in[:], t["a_state"], "a_params")
            load(ch_in[:], t["a_chan"], "a_params")
            load(ch_dt, t["a_chan_dt"], "a_params")
            load(br_in[:], t["a_br"], "a_params")
            load(bi_in[:], t["a_bi"], "a_params")
            load(h0_in[:], t["a_h0"], "a_params")
            load(a_d[:], t["a_d"], "a_params")
            load(a_c[:], t["a_c"], "a_params")
            pool.wait_ge(S("a_z_lo"), WT)
            load(t["out_s5"], a_last[:], "a_stored")
            pool.wait_ge(S("a_stored"), 16)

            pool.wait_ge(merge_done, 65)
            load(x_res[:], t["x"], "res_landed")
            pool.wait_ge(S("y_ready"), 1)
            load(t["out_y"], acc[:], "y_stored")
            pool.wait_ge(S("y_stored"), 16)

        @block.scalar
        def _(act):
            def f(out, in_, func, sem, **kw):
                act.activation(out, in_, func, **kw).then_inc(sem if not isinstance(sem, str) else S(sem), 1)

            def split(stage, i, u0, n):
                for u in range(u0, u0 + n):
                    slot = u % SLOTS
                    nth = i * (UNITS[stage] // SLOTS) + ((UNIT0[stage] + u) // SLOTS + 1)
                    act.wait_ge(landed[slot], nth * 16)
                    act.wait_ge(slots_freed, at(stage, i, u) + 1)
                    f(w_hi[:, slot], raw[:, slot], ACT.Copy, hi_ready)

            def merge(stage, m):
                with act.Fori(0, 4) as i:
                    split(stage, i, 0, 3)
                    for d in range(4):
                        if d < 3:
                            split(stage, i, 3 * d + 3, 3)
                        wait_block(act, stage, i, 2 * d, 3 * d + 1)
                        act.wait_ge(merge_done, i * 4 + (16 * m + d))
                        f(gate_t[:], ps[:, 0, 0:T], ACT.Tanh, bank_free[0], scale=0.5)

            def norm(n, x, sq_, pre, landed_at):
                act.wait_ge(S(pre + "_landed"), landed_at)
                f(sq_, x, ACT.Square, pre + "_squared")
                act.wait_ge(S(pre + "_summed"), 1)
                f(sd[:, 0:n], ps[:, 2, 0:n], ACT.Sqrt, pre + "_sd", scale=1.0 / D_MODEL, bias=eps[:])

            act.wait_ge(S("ones_ready"), 1)
            sqv = lambda n: sq[:, 0:KT * n].rearrange("p (k t) -> p k t", k=KT)
            norm(N_MEM, acc[:, :, 0:N_MEM], sqv(N_MEM), "mem", 16)
            act.wait_ge(S("mem_normed"), 1)
            f(m_hi[:], acc[:, :, 0:N_MEM], ACT.Copy, "m_hi_ready")
            norm(T, acc[:], sqv(T), "x", 16)
            act.wait_ge(S("x_normed"), 1)
            f(h_hi[:], acc[:], ACT.Copy, "h_hi_ready")

            act.wait_ge(S("h_split"), 1)
            with act.Fori(0, 4) as i:
                split("E", i, 0, 4)
                for b in range(8):
                    if b < 6:
                        split("E", i, 4 + 2 * b, 2)
                    wait_block(act, "E", i, b, 2 * b + 1)
                    bank = b % 2
                    if b < 4:
                        if b == 0:
                            act.wait_ge(S("kv_stored"), i * 32)
                            act.wait_ge(S("e_lo"), i)
                        f((kT if b < 2 else vT)[:, bank], ps[:, bank, 0:N_MEM], ACT.Copy, bank_free[bank])
                    elif b < 6:
                        f(eq[:, bank], ps[:, bank, 0:T], ACT.Copy, bank_free[bank], scale=HD ** -0.5)
                    else:
                        f(e_th[:, bank], ps[:, bank, 0:T], ACT.Tanh, "e_th", scale=0.5)
                act.wait_ge(S("e_vt"), i + 1)
                f(vm[:], ps[:, 6].rearrange("p (a b) -> p a b", a=2), ACT.Copy, "e_vm")
                act.wait_ge(S("e_scores"), i * 3 + 2)
                f(ssc[:], ps[:, 4, 0:2 * TS].rearrange("p (a b) -> p a b", a=2), ACT.Copy, "e_ssc")
                act.wait_ge(S("e_max"), i + 1)
                for tt in range(2):
                    f(prob[:, tt], ps[:, 3, tt * N_MEM:(tt + 1) * N_MEM], ACT.Exp, "e_exp",
                      bias=mx[:, tt:tt + 1], accum_out=rs[:, tt:tt + 1])
                f(prob[0:TS, 2], ps[0:TS, 5, 0:N_MEM], ACT.Exp, "e_exp",
                  bias=mx[0:TS, 2:3], accum_out=rs[0:TS, 2:3])
                act.wait_ge(S("e_pt"), i + 1)
                f(pT[:, :, 0:SEQ], ps[:, 2].rearrange("p (a t) -> p a t", a=2), ACT.Copy, "e_pT")
                f(pT[:, :, SEQ:T], ps[:, 4, 0:2 * TS].rearrange("p (a t) -> p a t", a=2), ACT.Copy, "e_pT")
                act.wait_ge(S("e_out"), i + 1)
                f(br_hi[:, bass.ds(i * 2, 2), :], e_out[:], ACT.Copy, "e_hi", scale=0.5)
            merge("mE", 0)

            act.wait_ge(merge_done, 16)
            act.wait_ge(S("d_abs_lam"), 1)
            f(d_sp[:, 0], d_sp[:, 1], ACT.Exp, "d_exp_lam", scale=-1.0)
            act.wait_ge(S("d_pad"), 1)
            with act.Fori(0, WT) as i:
                split("D", i, 0, 4)
                wait_block(act, "D", i, 0, 1)
                act.wait_ge(S("d_lo"), i)
                f(d_xp[:, 3:3 + SEQ], ps[:, 0, 0:SEQ], ACT.Copy, "d_xp")
                f(d_xs[:, :, 3:3 + NT], ps[:, 0, SEQ:T].rearrange("p (b t) -> p b t", t=NT), ACT.Copy, bank_free[0])
                wait_block(act, "D", i, 1, 3)
                f(d_th[:], ps[:, 1, 0:T], ACT.Tanh, "d_th", scale=0.5)
                act.wait_ge(S("d_gates"), i + 1)
                act.wait_ge(S("d_halved"), 1)
                f(d_r[:], ps[:, 2, 0:T], ACT.Tanh, "d_r", scale=0.5, bias=d_sp[:, 5, bass.ds(i, 1)])
                f(d_i[:], ps[:, 3, 0:T], ACT.Tanh, "d_i", scale=0.5, bias=d_sp[:, 6, bass.ds(i, 1)])
                act.wait_ge(S("d_L"), i + 1)
                f(d_a[:], d_L[:], ACT.Exp, "d_a")
                f(d_t[:], d_L[:], ACT.Tanh, "d_t", scale=-1.0)
                act.wait_ge(S("d_s"), i + 1)
                f(d_u[:], d_t[:], ACT.Sqrt, "d_sqrt")
                act.wait_ge(S("d_out"), i + 1)
                f(br_hi[:, bass.ds(i, 1), :], d_out[:].unsqueeze(1), ACT.Copy, "d_hi", scale=0.5)
            merge("mD", 1)

            def mix(i, nv):
                heads, v0 = heads_before(i, nv)

                def w(name, per=1, k=1):
                    act.wait_ge(S("g_" + name), heads * per + k)

                def wv(name, k):
                    act.wait_ge(S("g_" + name), v0 + k)

                w("vt")
                for tt in range(2):
                    f(g_vT[:, tt, 0:nv * P], ps[:, 2 + tt, 0:nv * P], ACT.Copy, "g_vT")
                f(g_vT[0:TS, 2, 0:nv * P], ps[0:TS, 4, 0:nv * P], ACT.Copy, "g_vT")
                w("D")
                f(g_X[:, 0:5, 0:SEQ], g_X[:, 0:5, 0:SEQ], ACT.Exp, "g_E")
                f(g_X[:, 5:9, :], g_X[:, 5:9, :], ACT.Exp, "g_E")
                f(g_eb[:], by_seq(g_b)[:, :, NT - 1], ACT.Exp, "g_E")
                w("kt")
                f(g_kT[:, 0:2], ps[:, 5, 0:2 * P].rearrange("p (a b) -> p a b", a=2), ACT.Copy, "g_kT")
                f(g_kT[0:TS, 2], ps[0:TS, 5, 2 * P:3 * P], ACT.Copy, "g_kT")
                f(g_att[:, 1], ps[:, 6, 0:P], ACT.Copy, "g_cross_out")
                w("o")
                for v in range(nv):
                    f(g_o2[:, v], ps[:, 2 + v, 0:T], ACT.Square, "g_sq")
                w("Sp_raw")
                f(g_Sp[:, 0:nv * P], ps[:, 4, 0:nv * P], ACT.Copy, "g_Sp")
                w("ssq")
                f(g_t[:, 2], ps[:, 7, 0:T], ACT.Ln, "g_ln_ms", scale=1.0 / (nv * P), bias=eps[:])
                w("ln_ms")
                f(g_t[:, 3], g_t[:, 2], ACT.Exp, "g_rstd", scale=-0.5)
                for v in range(nv):
                    wv("out", v + 1)
                    f(br_hi[:, bass.ds(i * nv + v, 1), :], g_o[:, v:v + 1], ACT.Copy, "g_hi")

            act.wait_ge(merge_done, 32)
            act.wait_ge(S("c_rT_raw"), 1)
            f(g_r[:], ps[0:GLA_RANK, 2, 0:T], ACT.Copy, "c_rT")
            act.wait_ge(S("lb_shift"), 1)
            f(g_lb[:, 2], g_lb[:, 1], ACT.Exp, "lb_exp")
            with act.Fori(0, 4) as i:
                split("C", i, 0, 4)
                for b in range(6):
                    if b < 4:
                        split("C", i, 4 + 2 * b, 2)
                    wait_block(act, "C", i, b, 2 * b + 1)
                    src = ps[:, b % 2, 0:T]
                    if b == 0:
                        act.wait_ge(S("g_lo"), i * 2)
                        act.wait_ge(S("g_new"), i)
                        act.wait_ge(S("g_stored"), i * 32)
                        f(g_q[:], src, ACT.Copy, bank_free[0], scale=P ** -0.5)
                    elif b == 1:
                        f(g_k[:], src, ACT.Copy, bank_free[1])
                    elif b < 4:
                        f(g_v[:, b - 2], src, ACT.Copy, bank_free[b % 2])
                    else:
                        f(g_e[:, b - 4], src, ACT.Exp, "g_ge", scale=-1.0)
                act.wait_ge(S("c_z"), i + 1)
                bias = g_cols[:, bass.ds(i + 4, 1)]
                f(g_t[:, 0], ps[:, 7, 0:T], ACT.Abs, "c_abs", bias=bias)
                f(g_t[:, 2], ps[:, 7, 0:T], ACT.Identity, "c_zb", bias=bias)
                act.wait_ge(S("c_abs"), i + 1)
                f(g_t[:, 1], g_t[:, 0], ACT.Exp, "c_w", scale=-1.0)
                act.wait_ge(S("c_w"), i + 1)
                f(g_t[:, 3], g_t[:, 1], ACT.Ln, "c_l1", bias=1.0)
                mix(i, 2)
            merge("mC", 2)

            act.wait_ge(merge_done, 48)
            with act.Fori(0, 8) as i:
                split("B", i, 0, 4)
                for b in range(4):
                    if b < 2:
                        split("B", i, 4 + 2 * b, 2)
                    wait_block(act, "B", i, b, 2 * b + 1)
                    src = ps[:, b % 2, 0:T]
                    if b == 0:
                        act.wait_ge(S("g_lo"), i + 8)
                        act.wait_ge(S("g_new"), i + 4)
                        act.wait_ge(S("g_stored"), i * 32 + 4 * 32)
                        f(g_q[:], src, ACT.Copy, bank_free[0])
                    elif b == 1:
                        f(g_t[:, 2], src, ACT.Copy, "b_zb")
                        f(g_t[:, 0], src, ACT.Abs, bank_free[1])
                        wait_taken(act, "B", i, 1)
                        f(g_t[:, 1], g_t[:, 0], ACT.Exp, "b_w", scale=-1.0)
                        act.wait_ge(S("b_w"), i + 1)
                        f(g_t[:, 3], g_t[:, 1], ACT.Ln, "b_l1", bias=1.0)
                    elif b == 2:
                        f(g_v[:, 0], src, ACT.Copy, bank_free[0])
                    else:
                        f(g_e[:, 0], src, ACT.Exp, "g_ge", scale=-1.0)
                act.wait_ge(S("b_kz"), i + 1)
                f(g_k[:], g_k[:], ACT.Exp, "b_kexp")
                f(g_t[:, 1], g_t[:, 0], ACT.Exp, "b_em")
                act.wait_ge(S("b_mixed"), i + 1)
                f(g_t[:, 3], g_t[:, 1], ACT.Ln, "b_ln")
                mix(i, 1)
            merge("mB", 3)

            act.wait_ge(merge_done, 64)
            act.wait_ge(S("a_params"), 16 * 8)
            f(st_dt, st_dt, ACT.Exp, "a_dt")
            f(ch_dt, ch_dt, ACT.Exp, "a_dt")
            act.wait_ge(S("a_theta"), 2)
            f(a_mag[:], st_a, ACT.Exp, "a_trig")
            f(a_cs[:, 1], st_th, ACT.Sin, "a_trig")
            f(st_abs, st_th, ACT.Abs, "a_trig")
            f(ch_mag, ch_a, ACT.Exp, "a_trig")
            f(ch_sin, ch_th, ACT.Sin, "a_trig")
            f(ch_abs, ch_th, ACT.Abs, "a_trig")
            act.wait_ge(S("a_trig"), 6)
            f(a_cs[:, 0], st_abs, ACT.Sin, "a_trig", scale=-1.0, bias=half_pi[:])
            f(ch_cos, ch_abs, ACT.Sin, "a_trig", scale=-1.0, bias=half_pi[:])
            act.wait_ge(S("a_set_up"), 1)
            with act.Fori(0, WT) as i:
                split("A", i, 0, 4)
                wait_block(act, "A", i, 0, 1)
                act.wait_ge(S("a_z_lo"), i)
                f(a_ud[:], ps[:, 0, 0:T], ACT.Copy, bank_free[0])
                wait_block(act, "A", i, 1, 3)
                f(a_th[:], ps[:, 1, 0:T], ACT.Tanh, "a_gate_th", scale=0.5)
                for pr in range(2):
                    act.wait_ge(S("a_scanned"), i * 4 + 2 * pr)
                    for j in range(2):
                        f(a_r[:, j], starts[:], ACT.Copy, "a_r", scale=a_mag[:, bass.ds(i * 4 + (2 * pr + j), 1)])
                act.wait_ge(S("a_inner"), i + 1)
                f(a_th[:], a_gs[:], ACT.Tanh, "a_tanh", scale=float(np.sqrt(2 / np.pi)))
                act.wait_ge(S("a_z2"), i + 1)
                f(z_hi[:, bass.ds(i, 1), :], a_th[:].unsqueeze(1), ACT.Copy, "a_z_hi", scale=0.5)
            with act.Fori(0, 2) as i:
                split("glu", i, 0, 4)
                for b in range(4):
                    wait_block(act, "glu", i, b, b)
                    act.wait_ge(S("glu_lo"), i * 4 + b)
                    f(a_th[:], ps[:, b % 2, 0:T], ACT.Tanh, bank_free[b % 2], scale=0.5)
                    act.wait_ge(S("glu_out"), i * 4 + (b + 1))
                    f(br_hi[:, bass.ds(i * 4 + b, 1), :], a_y[:].unsqueeze(1), ACT.Copy, "glu_hi", scale=0.125)
            merge("mA", 4)

            act.wait_ge(merge_done, 80)
            f(h_hi[:], acc[:], ACT.Copy, "o_hi_ready")
            act.wait_ge(S("o_split"), 1)
            with act.Fori(0, 8) as i:
                split("out", i, 0, 4)
                for b in range(2):
                    wait_block(act, "out", i, b, 2 * b + 1)
                    f(acc[:, bass.ds(i * 2 + b, 1), :], ps[:, b, 0:T].unsqueeze(1), ACT.Copy, bank_free[b])
            wait_taken(act, "out", 7, 0)
            wait_taken(act, "out", 7, 1)
            norm(T, acc[:], o_sq[:].rearrange("p (k t) -> p k t", k=KT), "res", 16)

        @block.vector
        def _(dve):
            ch = Chain(dve, S("dve_steps"))
            link = ch.link

            def sg(ins, name):
                ins.then_inc(S(name) if isinstance(name, str) else name, 1)

            def mul(out, a, b):
                return dve.tensor_tensor(out, a, b, ALU.mult)

            def add(out, a, b):
                return dve.tensor_tensor(out, a, b, ALU.add)

            def sub(out, a, b):
                return dve.tensor_tensor(out, a, b, ALU.subtract)

            def ts(out, a, s1, s2, op0, op1=ALU.bypass):
                return dve.tensor_scalar(out, a, s1, s2, op0, op1)

            def stt(out, a, s, b, op0, op1):
                return dve.scalar_tensor_tensor(out=out, in0=a, scalar=s, in1=b, op0=op0, op1=op1)

            def split(stage, i, u0, n):
                for u in range(u0, u0 + n):
                    slot = u % SLOTS
                    dve.wait_ge(hi_ready, at(stage, i, u) + 1)
                    sg(sub(w_lo[:, slot], raw[:, slot], w_hi[:, slot].bitcast(F32)), lo_ready)

            def low(dst, src, scale, high):
                return stt(dst, src, scale, high.bitcast(F32), ALU.mult, ALU.subtract)

            def merge(stage, m):
                with dve.Fori(0, 4) as i:
                    ch.enter(i, 0)
                    split(stage, i, 0, 3)
                    for d in range(4):
                        if d < 3:
                            split(stage, i, 3 * d + 3, 3)
                        wait_block(dve, stage, i, 2 * d + 1, 3 * d + 2)
                        wait_taken(dve, stage, i, 2 * d)
                        sg(stt(half_out[:], gate_t[:], 1.0, ps[:, 1, 0:T], ALU.add, ALU.mult), bank_free[1])
                        wait_taken(dve, stage, i, 2 * d + 1)
                        dst, src = acc[:, bass.ds(i * 4 + d, 1), :], half_out[:].unsqueeze(1)
                        if m == 0:
                            ins = ts(dst, src, 0.5, None, ALU.mult)
                        else:
                            ins = stt(dst, src, 0.5, dst, ALU.mult, ALU.add)
                        sg(ins, merge_done)
                        dve.wait_ge(merge_done, i * 4 + (16 * m + d + 1))
                ch.leave(4)

            def norm(n, x, sq_, pre, gains):
                dve.wait_ge(S(pre + "_squared"), 1)
                sg(dve.tensor_reduce(half_out[:, 0:n], sq_.rearrange("p k t -> p t k"), AX.X, ALU.add), pre + "_ksum")
                dve.wait_ge(S(pre + "_sd"), 1)
                link(dve.reciprocal(rstd[:, 0:n], sd[:, 0:n]))
                link(mul(x, x, rstd[:, 0:n].unsqueeze(1).to_broadcast([P, KT, n])))
                dve.wait_ge(S("norms_landed"), 16)
                return mul(x, x, norm_cols[:, gains, :].unsqueeze(2).to_broadcast([P, KT, n]))

            sqv = lambda n: sq[:, 0:KT * n].rearrange("p (k t) -> p k t", k=KT)
            sg(norm(N_MEM, acc[:, :, 0:N_MEM], sqv(N_MEM), "mem", 2), "mem_normed")
            dve.wait_ge(S("m_hi_ready"), 1)
            sg(sub(m_lo[:], acc[:, :, 0:N_MEM], m_hi[:].bitcast(F32)), "m_split")
            sg(norm(T, acc[:], sqv(T), "x", 0), "x_normed")
            dve.wait_ge(S("h_hi_ready"), 1)
            sg(sub(h_lo[:], acc[:], h_hi[:].bitcast(F32)), "h_split")

            with dve.Fori(0, 4) as i:
                ch.enter(i, LINKS["E"])
                split("E", i, 0, 16)
                for b in range(2):
                    dve.wait_ge(S("e_th"), i * 2 + (b + 1))
                    sg(stt(e_gate[:, b], e_th[:, b], 1.0, ps[:, b, 0:T], ALU.add, ALU.mult), bank_free[b])
                dve.wait_ge(S("e_scores"), i * 3 + 3)
                link(dve.tensor_reduce(mx[:, 0:2], ps[:, 3].rearrange("p (a m) -> p a m", a=2), AX.X, ALU.max))
                link(dve.tensor_reduce(mx[0:TS, 2:3], ps[0:TS, 5, 0:N_MEM], AX.X, ALU.max))
                link(ts(mx[:, 0:2], mx[:, 0:2], -1.0, None, ALU.mult))
                sg(ts(mx[0:TS, 2:3], mx[0:TS, 2:3], -1.0, None, ALU.mult), "e_max")
                dve.wait_ge(S("e_exp"), i * 3 + 3)
                link(dve.reciprocal(rs[:, 0:2], rs[:, 0:2]))
                link(dve.reciprocal(rs[0:TS, 2:3], rs[0:TS, 2:3]))
                for tt in range(2):
                    sg(ts(prob[:, tt], prob[:, tt], rs[:, tt:tt + 1], None, ALU.mult), "e_prob")
                sg(ts(prob[0:TS, 2], prob[0:TS, 2], rs[0:TS, 2:3], None, ALU.mult), "e_prob")
                dve.wait_ge(S("e_o"), i + 1)
                wait_taken(dve, "E", i, 6)
                wait_taken(dve, "E", i, 7)
                sg(mul(e_out[:], ps[:, 6:8, 0:T], e_gate[:]), "e_out")
                dve.wait_ge(S("e_hi"), i + 1)
                dve.wait_ge(S("e_out"), i + 1)
                sg(low(br_lo[:, bass.ds(i * 2, 2), :], e_out[:], 0.5, br_hi[:, bass.ds(i * 2, 2), :]), "e_lo")
            ch.leave(4)
            merge("mE", 0)

            dve.wait_ge(S("d_params"), 48)
            lam = d_cols[:, 7]
            link(ts(d_sp[:, 2], lam, -1.0, 0.0, ALU.mult, ALU.max))
            link(ts(d_sp[:, 3], lam, 0.0, None, ALU.max))
            sg(add(d_sp[:, 1], d_sp[:, 2], d_sp[:, 3]), "d_abs_lam")
            sg(ts(d_sp[:, 5:7], d_cols[:, 5:7], 0.5, None, ALU.mult), "d_halved")
            dve.wait_ge(S("d_exp_lam"), 1)
            y, z, z2, poly = d_sp[:, 0], d_sp[:, 1], d_sp[:, 3], d_sp[:, 4]
            link(ts(z, y, 2.0, None, ALU.add))
            link(dve.reciprocal(z, z))
            link(mul(z, z, y))
            link(mul(z2, z, z))
            link(ts(poly, z2, 1.0 / 17, 1.0 / 15, ALU.mult, ALU.add))
            for odd in (13, 11, 9, 7, 5, 3, 1):
                link(mul(poly, poly, z2))
                link(ts(poly, poly, 1.0 / odd, None, ALU.add))
            link(mul(poly, poly, z))
            link(stt(poly, poly, 2.0, d_sp[:, 2], ALU.mult, ALU.add))
            link(ts(d_sp[:, 7], poly, -LRU_C / 2, None, ALU.mult))
            with dve.Fori(0, WT) as i:
                ch.enter(i, LINKS["D"])
                split("D", i, 0, 4)
                wait_taken(dve, "D", i, 0)
                link(dve.tensor_copy(d_xs[:, :, 0:3], d_cbuf[:, bass.ds(i, 1)].rearrange("p a b c -> p (a b) c")))
                xp, xs = xc[:, 0:SEQ], by_seq(xc)
                for j in range(4):
                    w = d_cols[:, j, bass.ds(i, 1)]
                    if j == 0:
                        bias = d_cols[:, 4, bass.ds(i, 1)]
                        link(ts(xp, d_xp[:, 0:SEQ], w, bias, ALU.mult, ALU.add))
                        link(ts(xs, d_xs[:, :, 0:NT], w, bias, ALU.mult, ALU.add))
                    else:
                        link(stt(xp, d_xp[:, j:j + SEQ], w, xp, ALU.mult, ALU.add))
                        ins = stt(xs, d_xs[:, :, j:j + NT], w, xs, ALU.mult, ALU.add)
                        link(ins) if j < 3 else sg(ins, "d_xc")
                link(dve.tensor_copy(d_clast[:, bass.ds(i, 1), 0:1, :].rearrange("p a b c -> p (a b) c"),
                                     d_xp[:, SEQ:SEQ + 3].unsqueeze(1)))
                link(dve.tensor_copy(d_clast[:, bass.ds(i, 1), 1:N_SEQ, :].rearrange("p a b c -> p (a b) c"),
                                     d_xs[:, :, NT:NT + 3]))
                dve.wait_ge(S("d_th"), i + 1)
                sg(stt(d_gate[:], d_th[:], 1.0, ps[:, 1, 0:T], ALU.add, ALU.mult), bank_free[1])
                dve.wait_ge(S("d_r"), i + 1)
                sg(ts(d_L[:], d_r[:], 1.0, d_sp[:, 7, bass.ds(i, 1)], ALU.add, ALU.mult), "d_L")
                dve.wait_ge(S("d_i"), i + 1)
                link(stt(d_i[:], d_i[:], 1.0, xc[:], ALU.add, ALU.mult))
                dve.wait_ge(S("d_a"), i + 1)
                link(mul(d_r[:], d_a[:], d_a[:]))
                dve.wait_ge(S("d_t"), i + 1)
                sg(stt(d_t[:], d_r[:], 1.0, d_t[:], ALU.add, ALU.mult), "d_s")
                dve.wait_ge(S("d_sqrt"), i + 1)
                link(stt(d_u[:], d_i[:], 0.5, d_u[:], ALU.mult, ALU.mult))
                link(mul(d_inj[:], by_seq(d_a)[:, :, 0], d_h0[:, bass.ds(i, 1)].rearrange("p a b -> p (a b)")))
                link(add(by_seq(d_u)[:, :, 0], by_seq(d_u)[:, :, 0], d_inj[:]))
                link(mul(d_a[:], d_a[:], starts[:]))
                link(dve.tensor_tensor_scan(d_hseq[:], d_a[:], d_u[:], 0.0, ALU.mult, ALU.add))
                link(dve.tensor_copy(d_hlast[:, bass.ds(i, 1), 0:1], d_hseq[:, SEQ - 1:SEQ].unsqueeze(1)))
                link(dve.tensor_copy(d_hlast[:, bass.ds(i, 1), 1:N_SEQ], by_seq(d_hseq)[:, :, NT - 1].unsqueeze(1)))
                sg(mul(d_out[:], d_hseq[:], d_gate[:]), "d_out")
                dve.wait_ge(S("d_hi"), i + 1)
                dve.wait_ge(S("d_out"), i + 1)
                sg(low(br_lo[:, bass.ds(i, 1), :], d_out[:].unsqueeze(1), 0.5, br_hi[:, bass.ds(i, 1), :]), "d_lo")
            ch.leave(WT)
            merge("mD", 1)

            def silu(nth, v, bank):
                dve.wait_ge(S("g_ge"), nth)
                e = g_e[:, v]
                link(ts(e, e, 1.0, None, ALU.add))
                link(dve.reciprocal(e, e))
                sg(mul(g_gs[:, v], e, ps[:, bank, 0:T]), bank_free[bank])

            def halves(ap, h):
                n = T if 2 * h <= NT else SEQ
                return ap[:, 0:n].rearrange("p (b two h) -> p b two h", two=2, h=h), n // (2 * h)

            def mix(i, nv):
                heads, v0 = heads_before(i, nv)

                def w(name, per=1, k=1):
                    dve.wait_ge(S("g_" + name), heads * per + k)

                def wv(name, k):
                    dve.wait_ge(S("g_" + name), v0 + k)

                link(dve.tensor_tensor_scan(g_b[:], chunks[:], g_g[:], 0.0, ALU.mult, ALU.add))
                for l, h in enumerate(HALVES):
                    (bv, n), (xv, _) = halves(g_b, h), halves(g_X[:, l], h)
                    mid = bv[:, :, 0, h - 1:h].to_broadcast([P, n, h])
                    if h == CHUNK:
                        dve.tensor_copy(xv[:, :, 1], bv[:, :, 1])
                    else:
                        sub(xv[:, :, 1], bv[:, :, 1], mid)
                    sub(xv[:, :, 0], mid, bv[:, :, 0])
                c = lambda n: slice(n * CHUNK, (n + 1) * CHUNK)
                last = lambda n: g_b[:, (n + 1) * CHUNK - 1:(n + 1) * CHUNK]
                cross, final = g_X[:, CROSS], g_X[:, FINAL]
                dve.tensor_copy(cross[:, c(2)], g_b[:, c(2)])
                ts(cross[:, c(3)], g_b[:, c(3)], last(2), None, ALU.add)
                dve.tensor_copy(cross[:, SEQ:T], g_b[:, SEQ:T])
                ts(cross[:, c(1)], g_b[:, c(1)], last(1), -1.0, ALU.subtract, ALU.mult)
                ts(final[:, c(2)], g_b[:, c(2)], last(2), -1.0, ALU.subtract, ALU.mult)
                ts(final[:, c(3)], g_b[:, c(3)], last(3), -1.0, ALU.subtract, ALU.mult)
                sub(by_seq(final), by_seq(g_b)[:, :, NT - 1:NT].to_broadcast([P, NB, NT]), by_seq(g_b))
                link(add(g_bb[:], last(2), last(3)))
                link(ts(cross[:, c(0)], g_X[:, 0, c(0)], last(1), None, ALU.add))
                ts(final[:, c(2)], final[:, c(2)], last(3), None, ALU.add)
                sg(ts(final[:, 0:2 * CHUNK], cross[:, 0:2 * CHUNK], g_bb[:], None, ALU.add), "g_D")
                w("E", 3, 3)
                for l, h in enumerate(HALVES):
                    (xv, _), (qv, _), (kv, _) = halves(g_X[:, l], h), halves(g_q, h), halves(g_k, h)
                    mul(xv[:, :, 1], xv[:, :, 1], qv[:, :, 1])
                    mul(xv[:, :, 0], xv[:, :, 0], kv[:, :, 0])
                mul(cross[:, 0:P], cross[:, 0:P], g_k[:, 0:P])
                mul(cross[:, P:T], cross[:, P:T], g_q[:, P:T])
                sg(mul(final, final, g_k[:]), "g_X")
                for n in range(2):
                    w("levels", 3, 1 + 2 * n)
                    link(mul(g_prod[:].rearrange("p l t -> p (l t)"), ps[:, 2:4].rearrange("p a t -> p (a t)"),
                             levels[:].rearrange("p l t -> p (l t)")))
                    sg(dve.tensor_reduce(g_att[:, 2 * n], g_prod[:].rearrange("p l t -> p t l"), AX.X, ALU.add), "g_att")
                    w("att", 3, 1 + 2 * n)
                    if n == 0:
                        w("levels", 3, 2)
                        own = g_prod[0:TS, 0:3, 0:TS]
                        link(mul(own, ps[0:TS, 4, 0:3 * TS].rearrange("p (l t) -> p l t", t=TS), levels[0:TS, 5:8, 0:TS]))
                        sg(dve.tensor_reduce(g_atts[:], own.rearrange("p l t -> p t l"), AX.X, ALU.add), "g_att")
                        w("att", 3, 2)

                def new_states(half):
                    n = NB // nv
                    wv("up", half + 1)
                    if half == 0:
                        w("o")
                    for b in range(n):
                        s = g_S0[:, half * n + b, 0:nv * P]
                        ins = stt(s, s, g_eb[:, half * n + b:half * n + b + 1], up[:, b * nv * P:(b + 1) * nv * P],
                                  ALU.mult, ALU.add)
                    sg(ins, "g_new" if half == nv - 1 else "g_half_new")

                def own_values(half):
                    n = NB // nv
                    if half:
                        wv("up", half)
                    sg(mul(g_vm[:].rearrange("p (b v) -> p b v", v=nv * P),
                           g_vT[0:TS, 2, 0:nv * P].unsqueeze(1).to_broadcast([TS, n, nv * P]),
                           in_seq[:, half * n:(half + 1) * n].unsqueeze(2).to_broadcast([TS, n, nv * P])), "g_vm")

                w("vT", 3, 3)
                own_values(0)
                new_states(0)
                if nv == 2:
                    own_values(1)
                w("rstd")
                for v in range(nv):
                    link(mul(g_o[:, v], ps[:, 2 + v, 0:T], g_t[:, 3]))
                    gain = g_cols[:, v:v + 1] if nv == 2 else g_cols[:, 2:3]
                    sg(stt(g_o[:, v], g_o[:, v], gain, g_gs[:, v], ALU.mult, ALU.mult), "g_out")
                if nv == 2:
                    new_states(1)
                for v in range(nv):
                    wv("out", v + 1)
                    wv("hi", v + 1)
                    sg(low(br_lo[:, bass.ds(i * nv + v, 1), :], g_o[:, v:v + 1], 1.0,
                           br_hi[:, bass.ds(i * nv + v, 1), :]), "g_lo")

            dve.wait_ge(S("g_params"), 48)
            sg(sub(g_lb[:, 1], g_lb[:, 0], g_lb[:, 0]), "lb_shift")
            dve.wait_ge(S("lb_exp"), 1)
            link(dve.reciprocal(g_lb[:, 3], g_lb[:, 2]))
            link(mul(g_lb[:, 3], g_lb[:, 3], g_lb[:, 2]))
            link(sub(g_lb[:, 0], g_lb[:, 3], g_lb[:, 3]))
            link(ts(g_lb[:, 1], g_lb[:, 0], -1.0, 1.0, ALU.mult, ALU.add))
            with dve.Fori(0, 4) as i:
                ch.enter(i, LINKS["C"])
                split("C", i, 0, 12)
                silu(i * 2 + 1, 0, 0)
                silu(i * 2 + 2, 1, 1)
                dve.wait_ge(S("c_l1"), i + 1)
                link(stt(g_g[:], g_t[:, 2], 0.0, g_t[:, 3], ALU.min, ALU.subtract))
                link(ts(g_g[:], g_g[:], 1.0 / 16.0, None, ALU.mult))
                mix(i, 2)
            ch.leave(4)
            merge("mC", 2)

            with dve.Fori(0, 8) as i:
                ch.enter(i, LINKS["B"])
                split("B", i, 0, 8)
                silu(i + 9, 0, 1)
                dve.wait_ge(S("b_l1"), i + 1)
                link(stt(g_g[:], g_t[:, 2], 0.0, g_t[:, 3], ALU.min, ALU.subtract))
                link(sub(g_k[:], g_g[:], g_t[:, 2]))
                sg(ts(g_t[:, 0], g_g[:], -1.0, 40.0, ALU.mult, ALU.min), "b_kz")
                bound, rest = g_lb[:, 0, bass.ds(i, 1)], g_lb[:, 1, bass.ds(i, 1)]
                dve.wait_ge(S("b_em"), i + 1)
                sg(ts(g_t[:, 1], g_t[:, 1], bound, rest, ALU.mult, ALU.add), "b_mixed")
                link(ts(g_k[:], g_k[:], rest, None, ALU.mult))
                dve.wait_ge(S("b_ln"), i + 1)
                link(add(g_g[:], g_g[:], g_t[:, 3]))
                mix(i, 1)
            ch.leave(8)
            merge("mB", 3)

            dve.wait_ge(S("a_params"), 16 * 8)
            dve.wait_ge(S("a_dt"), 2)
            for lr, li, dt, a, th, n in ((st_in[:, 0], st_in[:, 1], st_dt, st_a, st_th, st_n),
                                         (ch_in[:, 0], ch_in[:, 1], ch_dt.unsqueeze(2).to_broadcast([P, WT, 64]),
                                          ch_a, ch_th, ch_n)):
                link(mul(a, lr, dt))
                link(mul(th, li, dt))
                link(ts(n, th, float(1 / (2 * np.pi)), ROUND, ALU.mult, ALU.add))
                link(ts(n, n, -ROUND, None, ALU.add))
                for part in TWO_PI:
                    link(stt(th, n, -part, th, ALU.mult, ALU.add))
                sg(ts(th, th, -PI_IN, PI_IN, ALU.max, ALU.min), "a_theta")
            dve.wait_ge(S("a_trig"), 8)
            lr, li = ch_in[:, 0], ch_in[:, 1]
            link(mul(ch_cos, ch_cos, ch_mag))
            link(mul(ch_sin, ch_sin, ch_mag))
            link(ts(ch_cos, ch_cos, -1.0, None, ALU.add))
            link(mul(ch_a, lr, lr))
            link(mul(ch_n, li, li))
            link(add(ch_a, ch_a, ch_n))
            link(dve.reciprocal(ch_a, ch_a))
            link(mul(ch_th, ch_cos, lr))
            link(mul(ch_n, ch_sin, li))
            link(add(ch_th, ch_th, ch_n))
            link(mul(ch_th, ch_th, ch_a))
            link(mul(ch_abs, ch_sin, lr))
            link(mul(ch_n, ch_cos, li))
            link(sub(ch_abs, ch_abs, ch_n))
            link(mul(ch_abs, ch_abs, ch_a))
            link(mul(ch_mag, ch_th, br_in[:]))
            link(mul(ch_n, ch_abs, bi_in[:]))
            link(sub(a_bb[:, 0], ch_mag, ch_n))
            link(mul(ch_mag, ch_th, bi_in[:]))
            link(mul(ch_n, ch_abs, br_in[:]))
            link(add(a_bb[:, 1], ch_mag, ch_n))
            link(mul(st_a, a_mag[:], a_cs[:, 0]))
            link(mul(st_n, a_mag[:], a_cs[:, 1]))
            ar, ai = (x.unsqueeze(2).to_broadcast([P, 32, NB]) for x in (st_a, st_n))
            link(mul(a_inj[:, 0], h0_in[:, 0], ar))
            link(mul(st_tmp, h0_in[:, 1], ai))
            link(sub(a_inj[:, 0], a_inj[:, 0], st_tmp))
            link(mul(a_inj[:, 1], h0_in[:, 1], ar))
            link(mul(st_tmp, h0_in[:, 0], ai))
            link(add(a_inj[:, 1], a_inj[:, 1], st_tmp))
            link(ts(a_c[:, 1], a_c[:, 1], -1.0, None, ALU.mult))
            for table in (a_p, a_q):
                link(dve.memset(table[:, 0, :, 0:1], 1.0))
                link(dve.memset(table[:, 1, :, 0:1], 0.0))
                for m in (1, 2, 4, 8):
                    old = table[:, :, :, 0:m]
                    new = table[:, :, :, m:2 * m]
                    c, s = (a_cs[:, k].unsqueeze(1).unsqueeze(3).to_broadcast([P, 2, 32, m]) for k in range(2))
                    t1, t2 = tab_t1[:, :, :, 0:m], tab_t2[:, :, :, 0:m]
                    link(mul(t1, old, c))
                    link(mul(t2, old, s))
                    link(sub(new[:, 0], t1[:, 0], t2[:, 1]))
                    link(add(new[:, 1], t1[:, 1], t2[:, 0]))
                    link(mul(st_a, a_cs[:, 0], a_cs[:, 0]))
                    link(mul(st_n, a_cs[:, 1], a_cs[:, 1]))
                    link(stt(a_cs[:, 1], a_cs[:, 0], 2.0, a_cs[:, 1], ALU.mult, ALU.mult))
                    link(sub(a_cs[:, 0], st_a, st_n))
            sg(dve.memset(zero[:], 0.0), "a_set_up")
            dve.wait_ge(S("a_set_up"), 1)
            with dve.Fori(0, WT) as i:
                ch.enter(i, LINKS["A"])
                split("A", i, 0, 4)
                for k in range(2):
                    sg(mul(a_B[:, k], a_bb[:, k, bass.ds(i, 1), :].to_broadcast([P, 8, 64]),
                           in_group[:].unsqueeze(2).to_broadcast([P, 8, 64])), "a_B")
                for k in range(2):
                    sg(mul(a_C[:, k].rearrange("p j (g o) -> p j g o", g=8),
                           a_c[:, k, bass.ds(i * 4, 4), :].unsqueeze(2).to_broadcast([P, 4, 8, 16]),
                           st_group[:].unsqueeze(3).to_broadcast([P, 4, 8, 16])), "a_C")
                for pr in range(2):
                    for j in range(2):
                        tile = bass.ds(i * 4 + (2 * pr + j), 1)
                        p = a_p[:, :, tile, :].to_broadcast([P, 2, 16, 16])
                        q = [a_q[:, k, tile, :].rearrange("p a q -> p (a q)").unsqueeze(1).unsqueeze(3).to_broadcast([P, 2, 16, 16])
                             for k in range(2)]
                        t1, t2 = (x.rearrange("p a b t -> p (a b t)")[:, 0:512].rearrange(
                            "p (a q r) -> p a q r", a=2, q=16) for x in (a_t1[:], a_t2[:]))
                        link(mul(t1, p, q[0]))
                        link(mul(t2, p, q[1]))
                        row = lambda k: a_P[:, k, j, 0:SEQ].rearrange("p (q r) -> p q r", q=16)
                        link(sub(row(0), t1[:, 0], t2[:, 1]))
                        link(add(row(1), t1[:, 1], t2[:, 0]))
                    for k in range(2):
                        link(dve.tensor_copy(a_P[:, k, :, SEQ:T].rearrange("p j (b t) -> p j b t", t=NT),
                                             a_P[:, k, :, 0:NT].unsqueeze(2).to_broadcast([P, 2, NB, NT])))
                    cos, sin = (a_P[:, k].unsqueeze(1).to_broadcast([P, 2, 2, T]) for k in range(2))
                    dve.wait_ge(S("a_x"), i * 2 + (pr + 1))
                    x = ps[:, 2:6, 0:T].rearrange("p (k j) t -> p k j t", k=2)
                    link(mul(a_t1[:], x, cos))
                    sg(mul(a_t2[:], x, sin), "a_x_used")
                    dve.wait_ge(S("a_x_used"), i * 2 + (pr + 1))
                    dve.wait_ge(S("a_y_part"), i * 2 + pr)
                    link(add(a_m[:, 0], a_t1[:, 0], a_t2[:, 1]))
                    link(sub(a_m[:, 1], a_t1[:, 1], a_t2[:, 0]))
                    for k in range(2):
                        first = a_m[:, k, :, SEQ:T].rearrange("p j (b t) -> p j b t", t=NT)[:, :, :, 0]
                        link(add(first, first, a_inj[:, k, bass.ds(i * 4 + 2 * pr, 2), :]))
                    dve.wait_ge(S("a_r"), i * 4 + (2 * pr + 2))
                    for k in range(2):
                        sg(dve.tensor_tensor_scan(a_g[:, k].rearrange("p j t -> p (j t)"), a_r[:].rearrange("p j t -> p (j t)"),
                                                  a_m[:, k].rearrange("p j t -> p (j t)"), 0.0, ALU.mult, ALU.add), "a_scanned")
                    dve.wait_ge(S("a_scanned"), i * 4 + (2 * pr + 2))
                    link(mul(a_t1[:], a_g[:], cos))
                    link(mul(a_t2[:], a_g[:], sin))
                    link(sub(a_m[:, 0], a_t1[:, 0], a_t2[:, 1]))
                    sg(add(a_m[:, 1], a_t1[:, 1], a_t2[:, 0]), "a_H")
                    dve.wait_ge(S("a_H"), i * 2 + (pr + 1))
                    tiles = bass.ds(i * 4 + 2 * pr, 2)
                    link(dve.tensor_copy(a_last[:, :, tiles, 0:1], a_m[:, :, :, SEQ - 1:SEQ]))
                    for k in range(2):
                        link(ts(a_last[:, k, tiles, 1:N_SEQ],
                                a_m[:, k, :, SEQ:T].rearrange("p j (b t) -> p j b t", t=NT)[:, :, :, NT - 1], 1.0, None, ALU.mult))
                dve.wait_ge(S("a_gate_th"), i + 1)
                sg(stt(a_gate[:], a_th[:], 1.0, ps[:, 1, 0:T], ALU.add, ALU.mult), bank_free[1])
                dve.wait_ge(S("a_y_part"), i * 2 + 2)
                link(stt(a_y[:], a_ud[:], a_d[:, bass.ds(i, 1)], ps[:, 6, 0:T], ALU.mult, ALU.add))
                link(mul(a_gs[:], a_y[:], a_y[:]))
                link(ts(a_gs[:], a_gs[:], 0.044715, 1.0, ALU.mult, ALU.add))
                sg(mul(a_gs[:], a_gs[:], a_y[:]), "a_inner")
                dve.wait_ge(S("a_tanh"), i + 1)
                sg(stt(a_th[:], a_th[:], 1.0, a_y[:], ALU.add, ALU.mult), "a_z2")
                dve.wait_ge(S("a_z2"), i + 1)
                link(mul(zg[:, bass.ds(i, 1), :], a_th[:].unsqueeze(1), a_gate[:].unsqueeze(1)))
                dve.wait_ge(S("a_z_hi"), i + 1)
                sg(low(z_lo[:, bass.ds(i, 1), :], a_th[:].unsqueeze(1), 0.5, z_hi[:, bass.ds(i, 1), :]), "a_z_lo")
            ch.leave(WT)
            with dve.Fori(0, 2) as i:
                split("glu", i, 0, 4)
                for b in range(4):
                    wait_taken(dve, "glu", i, b)
                    sg(stt(a_y[:].unsqueeze(1), a_th[:].unsqueeze(1), 1.0, zg[:, bass.ds(i * 4 + b, 1), :], ALU.add, ALU.mult), "glu_out")
                    dve.wait_ge(S("glu_hi"), i * 4 + (b + 1))
                    dve.wait_ge(S("glu_out"), i * 4 + (b + 1))
                    br = bass.ds(i * 4 + b, 1)
                    sg(low(br_lo[:, br, :], a_y[:].unsqueeze(1), 0.125, br_hi[:, br, :]), "glu_lo")
                    dve.wait_ge(S("glu_lo"), i * 4 + (b + 1))
            merge("mA", 4)

            dve.wait_ge(S("o_hi_ready"), 1)
            sg(sub(h_lo[:], acc[:], h_hi[:].bitcast(F32)), "o_split")
            with dve.Fori(0, 8) as i:
                split("out", i, 0, 4)
            link(norm(T, acc[:], o_sq[:].rearrange("p (k t) -> p k t", k=KT), "res", 1))
            sg(add(acc[:], acc[:], x_res[:]), "y_ready")

        @block.tensor
        def _(pe):
            def mm(out, a, b, start=True, stop=True):
                return pe.matmul(out, a, b, start=start, stop=stop)

            def sg(ins, name):
                ins.then_inc(S(name) if isinstance(name, str) else name, 1)

            def project(stage, i, b, u0, n_units, x_hi, x_lo, n):
                bank = b % 2
                pe.wait_ge(bank_free[bank], earlier(stage, i, b))
                for u in range(n_units):
                    slot = (u0 + u) % SLOTS
                    pe.wait_ge(lo_ready, at(stage, i, u0 + u) + 1)
                    for k in range(UK):
                        kt = u * UK + k
                        first, last = kt == 0, kt == n_units * UK - 1
                        mm(ps[:, bank, 0:n], w_hi[:, slot, k], x_hi[:, kt], first, False)
                        mm(ps[:, bank, 0:n], w_lo[:, slot, k], x_hi[:, kt], False, False)
                        ins = mm(ps[:, bank, 0:n], w_hi[:, slot, k], x_lo[:, kt], False, last)
                    sg(ins, slots_freed)

            def merge(stage):
                with pe.Fori(0, 4) as i:
                    for d in range(4):
                        project(stage, i, 2 * d, 3 * d, 2, h_hi, h_lo, T)
                        project(stage, i, 2 * d + 1, 3 * d + 2, 1, br_hi, br_lo, T)

            def sum_channels(pre, n):
                pe.wait_ge(S(pre + "_ksum"), 1)
                sg(mm(ps[:, 2, 0:n], ones[:], half_out[:, 0:n]), pre + "_summed")

            pe.wait_ge(S("ones_ready"), 1)
            sum_channels("mem", N_MEM)
            sum_channels("x", T)
            pe.wait_ge(S("masks_ready"), 1)
            pe.wait_ge(S("h_split"), 1)

            with pe.Fori(0, 4) as i:
                for b in range(8):
                    x = (m_hi, m_lo, N_MEM) if b < 4 else (h_hi, h_lo, T)
                    project("E", i, b, 2 * b, 2, *x)
                wait_taken(pe, "E", i, 3)
                pe.wait_ge(S("e_lo"), i)
                for mt in range(2):
                    for ct in range(2):
                        at_ = mt * HD + ct * P
                        ins = pe.transpose(ps[:, 6, at_:at_ + P], vT[:, ct, mt * P:(mt + 1) * P], ident[:])
                sg(ins, "e_vt")
                wait_taken(pe, "E", i, 4)
                wait_taken(pe, "E", i, 5)
                for tt in range(2):
                    for dt in range(2):
                        ins = mm(ps[:, 3, tt * N_MEM:(tt + 1) * N_MEM], eq[:, dt, tt * P:(tt + 1) * P], kT[:, dt], dt == 0, dt == 1)
                sg(ins, "e_scores")
                pe.wait_ge(S("kc_landed"), i * 16 + 16)
                for mt in range(2):
                    for b in range(NB):
                        for dt in range(2):
                            ins = mm(ps[:, 4, mt * TS + b * NT:mt * TS + (b + 1) * NT], kc[:, dt, b, mt * P:(mt + 1) * P],
                                     eq[:, dt, SEQ + b * NT:SEQ + (b + 1) * NT], dt == 0, dt == 1)
                sg(ins, "e_scores")
                pe.wait_ge(S("e_ssc"), i + 1)
                for mt in range(2):
                    ins = pe.transpose(ps[0:TS, 5, mt * P:(mt + 1) * P], ssc[:, mt], ident[:])
                sg(ins, "e_scores")
                pe.wait_ge(S("e_prob"), i * 3 + 3)
                for mt in range(2):
                    for tt in range(2):
                        pe.transpose(ps[:, 2, mt * SEQ + tt * P:mt * SEQ + (tt + 1) * P], prob[:, tt, mt * P:(mt + 1) * P], ident[:])
                    ins = pe.transpose(ps[:, 4, mt * TS:(mt + 1) * TS], prob[0:TS, 2, mt * P:(mt + 1) * P], ident[0:TS, 0:TS])
                sg(ins, "e_pt")
                pe.wait_ge(S("e_pT"), i * 2 + 2)
                pe.wait_ge(S("e_vm"), i + 1)
                pe.wait_ge(S("vc_landed"), i * 16 + 16)
                for ct in range(2):
                    out = ps[:, 6 + ct]
                    for mt in range(2):
                        mm(out[:, 0:SEQ], vm[:, mt, ct * P:(ct + 1) * P], pT[:, mt, 0:SEQ], mt == 0, mt == 1)
                    for b in range(NB):
                        for mt in range(2):
                            seq = slice(SEQ + b * NT, SEQ + (b + 1) * NT)
                            ins = mm(out[:, seq], vc[:, mt, b, ct * P:(ct + 1) * P], pT[:, mt, seq], mt == 0, mt == 1)
                sg(ins, "e_o")
            pe.wait_ge(S("e_lo"), 4)
            merge("mE")

            with pe.Fori(0, WT) as i:
                for b in range(2):
                    project("D", i, b, 2 * b, 2, h_hi, h_lo, T)
                pe.wait_ge(S("d_xc"), i + 1)
                pe.wait_ge(S("d_w_landed"), i * 16 + 16)
                pe.wait_ge(S("d_i"), i)
                mm(ps[:, 2, 0:T], d_w[:, 0], xc[:])
                sg(mm(ps[:, 3, 0:T], d_w[:, 1], xc[:]), "d_gates")
            pe.wait_ge(S("d_lo"), WT)
            merge("mD")

            def mix(i, nv):
                heads, v0 = heads_before(i, nv)

                def w(name, per=1, k=1):
                    pe.wait_ge(S("g_" + name), heads * per + k)

                def wv(name, k):
                    pe.wait_ge(S("g_" + name), v0 + k)

                wv("lo", 0)
                for v in range(nv):
                    for tt in range(2):
                        pe.transpose(ps[:, 2 + tt, v * P:(v + 1) * P], g_v[:, v, tt * P:(tt + 1) * P], ident[:])
                    ins = pe.transpose(ps[0:TS, 4, v * P:(v + 1) * P], g_v[:, v, SEQ:T], ident[:])
                sg(ins, "g_vt")
                w("X")
                w("vT", 3, 3)
                lev = ps[:, 2:4].rearrange("p a (l t) -> p (a l) t", t=P)

                def pairs(tok):
                    for l in range(7):
                        mm(lev[:, l], g_X[:, l, tok], g_X[:, l, tok])
                    sg(mm(lev[:, DIAG], g_k[:, tok], g_q[:, tok]), "g_levels")

                pairs(slice(0, P))
                for n, (a, b) in enumerate(((g_X[:, 5], g_X[:, 5]), (g_X[:, 6], g_X[:, 6]), (g_k, g_q))):
                    ins = mm(ps[0:TS, 4, n * TS:(n + 1) * TS], a[:, SEQ:T], b[:, SEQ:T])
                sg(ins, "g_levels")
                mm(ps[:, 6, 0:P], g_X[:, CROSS, 0:P], g_X[:, CROSS, P:2 * P])
                for tt in range(2):
                    pe.transpose(ps[:, 5, tt * P:(tt + 1) * P], g_X[:, FINAL, tt * P:(tt + 1) * P], ident[:])
                sg(pe.transpose(ps[0:TS, 5, 2 * P:3 * P], g_X[:, FINAL, SEQ:T], ident[:]), "g_kt")
                w("att", 3, 1)
                pairs(slice(P, 2 * P))
                w("att", 3, 3)
                w("cross_out")
                pe.wait_ge(S("g_S0_landed"), heads * 16 + 16)
                for v in range(nv):
                    out, val = ps[:, 2 + v], lambda n: g_vT[:, n, v * P:(v + 1) * P]
                    mm(out[:, 0:2 * P], val(0), g_att[:, 0:2].rearrange("p a t -> p (a t)"), True, False)
                    mm(out[:, P:2 * P], val(1), g_att[:, 2], False, False)
                    mm(out[:, SEQ:T], val(2)[0:TS], g_atts[:], False, False)
                    for b in range(NB):
                        seq = slice(SEQ + b * NT, SEQ + (b + 1) * NT)
                        ins = mm(out[:, seq], g_S0[:, b, v * P:(v + 1) * P], g_X[:, CROSS, seq], False, b == NB - 1)
                sg(ins, "g_o")
                w("kT", 2, 2)
                mm(ps[:, 4, 0:nv * P], g_kT[:, 0], g_vT[:, 0, 0:nv * P], True, False)
                sg(mm(ps[:, 4, 0:nv * P], g_kT[:, 1], g_vT[:, 1, 0:nv * P], False, True), "g_Sp_raw")

                def updates(half):
                    wv("vm", half + 1)
                    if half:
                        w("half_new")
                    mm(ps[:, 5], g_kT[0:TS, 2], g_vm[:, 0:512])
                    sg(mm(ps[:, 6], g_kT[0:TS, 2], g_vm[:, 512:1024]), "g_up")

                updates(0)
                wv("sq", nv)
                for v in range(nv):
                    ins = mm(ps[:, 7, 0:T], ones[:], g_o2[:, v], v == 0, v == nv - 1)
                sg(ins, "g_ssq")
                if nv == 2:
                    updates(1)

            pe.wait_ge(S("g_params"), 48)
            for n, part in enumerate((h_hi, h_lo)):
                for k in range(KT):
                    ins = mm(ps[0:GLA_RANK, 2, 0:T], g_wr[:, k], part[:, k].bitcast(F32), n + k == 0, n == 1 and k == KT - 1)
            sg(ins, "c_rT_raw")
            pe.wait_ge(S("c_rT"), 1)
            with pe.Fori(0, 4) as i:
                for b in range(6):
                    project("C", i, b, 2 * b, 2, h_hi, h_lo, T)
                pe.wait_ge(S("c_wu_landed"), i * 16 + 16)
                pe.wait_ge(S("g_lo"), i * 2)
                sg(mm(ps[:, 7, 0:T], g_wu[:], g_r[:]), "c_z")
                wait_taken(pe, "C", i, 3)
                mix(i, 2)
            pe.wait_ge(S("g_lo"), 8)
            merge("mC")

            with pe.Fori(0, 8) as i:
                for b in range(4):
                    project("B", i, b, 2 * b, 2, h_hi, h_lo, T)
                wait_taken(pe, "B", i, 2)
                mix(i, 1)
            pe.wait_ge(S("g_lo"), 16)
            merge("mB")

            with pe.Fori(0, WT) as i:
                for b in range(2):
                    project("A", i, b, 2 * b, 2, h_hi, h_lo, T)
                wait_taken(pe, "A", i, 0)
                pe.wait_ge(S("a_B"), i * 2 + 2)
                pe.wait_ge(S("a_C"), i * 2 + 2)

                def inputs(pr):
                    pe.wait_ge(S("a_x_used"), i * 2 + pr)
                    for k in range(2):
                        for j in range(2):
                            lhsT = a_B[:, k, 2 * (2 * pr + j):2 * (2 * pr + j) + 2, :].rearrange("p g s -> p (g s)")
                            ins = mm(ps[:, 2 + 2 * k + j, 0:T], lhsT, a_ud[:])
                    sg(ins, "a_x")

                def outputs(pr):
                    pe.wait_ge(S("a_H"), i * 2 + (pr + 1))
                    for k in range(2):
                        for j in range(2):
                            ins = mm(ps[:, 6, 0:T], a_C[:, k, 2 * pr + j], a_m[:, k, j],
                                     pr + k + j == 0, pr + k + j == 3)
                    sg(ins, "a_y_part")

                inputs(0)
                inputs(1)
                outputs(0)
                outputs(1)
            pe.wait_ge(S("a_z_lo"), WT)
            with pe.Fori(0, 2) as i:
                for b in range(4):
                    project("glu", i, b, b, 1, z_hi, z_lo, T)
            pe.wait_ge(S("glu_lo"), WT)
            merge("mA")

            pe.wait_ge(S("o_split"), 1)
            with pe.Fori(0, 8) as i:
                for b in range(2):
                    project("out", i, b, 2 * b, 2, h_hi, h_lo, T)
            sum_channels("res", T)


SPLITS = (("a_x", W), ("a_g", W), ("b_q", W), ("b_f", W), ("b_i", W), ("b_g", W), ("c_q", W // 2), ("c_k", W // 2),
          ("c_v", W), ("c_r", GLA_RANK), ("c_g", W), ("d_x", W), ("d_g", W), ("e_q", W), ("e_g", W))


def blocks(w):
    rows, cols = w.shape
    return w.reshape(rows // (UK * P), UK, P, cols // P, P).transpose(3, 0, 2, 1, 4).reshape(cols // P, -1, P, UK * P)


def heads(n, *parts):
    return np.concatenate([p.reshape(n, -1, P, UK * P) for p in parts], axis=1).reshape(-1, P, UK * P)


def tiles(a):
    a = a.reshape(*a.shape[:-1], -1, P)
    return np.moveaxis(np.moveaxis(a, -1, 0), -1, 1)


def layout(x):
    x = {k: np.asarray(v) for k, v in x.items()}
    g = {k: v[0] for k, v in x.items() if k not in ("x_prompt", "x_sample", "mem_prompt")}
    at, win = 0, {}
    for name, width in SPLITS:
        win[name] = g["w_in"][:, at:at + width]
        at += width
    wb = {name: blocks(w) for name, w in win.items() if name != "c_r"}
    merge = [heads(KT, blocks(g["w_merge"][:, n * D_MODEL:(n + 1) * D_MODEL]), blocks(g["w_branch"][n])) for n in range(5)]
    stream = np.concatenate([
        heads(4, blocks(g["w_mem_k"]), blocks(g["w_mem_v"]), wb["e_q"], wb["e_g"]), merge[4],
        heads(WT, wb["d_x"], wb["d_g"]), merge[3],
        heads(4, wb["c_q"], wb["c_k"], wb["c_v"], wb["c_g"]), merge[2],
        heads(8, wb["b_q"], wb["b_f"], wb["b_i"], wb["b_g"]), merge[1],
        heads(WT, wb["a_x"], wb["a_g"]), heads(WT, blocks(g["s5_w_glu"])), merge[0],
        heads(KT, blocks(g["w_out"]))])
    tok = np.concatenate([x["x_prompt"][0], x["x_sample"].reshape(TS, D_MODEL)])

    def cache(a):
        return a.reshape(NB, N_MEM, 4, HD).transpose(2, 0, 1, 3)

    kc = cache(g["cache_mem_k"]).reshape(4, NB, N_MEM, 2, P).transpose(0, 4, 3, 1, 2)
    vc = cache(g["cache_mem_v"]).reshape(4, NB, 2, P, HD).transpose(0, 3, 2, 1, 4)
    states = lambda a: a.reshape(32, P, *a.shape[1:]).swapaxes(0, 1)
    flat = lambda a: a.reshape(-1, *a.shape[2:])
    rep = lambda a: np.repeat(a, 16, axis=0).reshape(WT, P, -1).swapaxes(0, 1)
    chan = lambda a: a.transpose(0, 2, 1).reshape(WT, P, 64).swapaxes(0, 1)
    out = {
        "w": stream,
        "mem": tiles(x["mem_prompt"][0]), "x": tiles(tok),
        "norms": np.stack([tiles(g[n]) for n in ("norm_pre", "norm_post", "mem_norm")], 1),
        "kc": kc, "vc": vc,
        "d_cols": np.stack([tiles(a) for a in (*g["conv_w"], g["conv_b"], g["lru_b_r"], g["lru_b_i"], g["lru_lam"])], 1),
        "d_cbuf": tiles(g["state_conv"]), "d_h0": tiles(g["state_rglru"]),
        "d_w": np.stack([g["lru_w_r"], g["lru_w_i"]], 2),
        "g_cols": np.concatenate([tiles(g["gla_norm"]), tiles(g["hg_norm"]), tiles(g["hg_norm"]), tiles(g["gla_b_up"])], 1),
        "lb": tiles(g["hg_lb_logits"]),
        "w_r": win["c_r"].reshape(KT, P, GLA_RANK).swapaxes(0, 1),
        "w_up": g["gla_w_up"].reshape(GLA_RANK, 4, P).swapaxes(0, 1),
        "gla": g["state_gla"].transpose(1, 2, 0, 3), "hgrn": g["state_hgrn"].transpose(1, 2, 0, 3),
        "a_state": np.stack([states(flat(g["s5_lam_re"])), states(flat(g["s5_lam_im"])),
                             states(np.repeat(g["s5_log_dt"], 64))], 1),
        "a_chan": np.stack([rep(g["s5_lam_re"]), rep(g["s5_lam_im"])], 1),
        "a_chan_dt": rep(g["s5_log_dt"][:, None])[:, :, 0],
        "a_br": chan(g["s5_b_re"]), "a_bi": chan(g["s5_b_im"]),
        "a_h0": np.stack([states(g[n].reshape(NB, -1).T) for n in ("state_s5_re", "state_s5_im")], 1),
        "a_d": tiles(g["s5_d"]),
        "a_c": np.stack([states(flat(g[n].transpose(0, 2, 1))) for n in ("s5_c_re", "s5_c_im")], 1),
    }
    return {k: np.ascontiguousarray(v) for k, v in out.items()}


OUTPUTS = {"out_y": (P, KT, T), "out_mem_k": (4, P, 2, N_MEM), "out_mem_v": (4, P, 2, N_MEM),
           "out_lru": (P, WT, N_SEQ), "out_conv": (P, WT, N_SEQ, 3),
           "out_gla_s": (4, P, NB, 256), "out_gla_p": (4, P, 256),
           "out_hg_s": (8, P, NB, P), "out_hg_p": (8, P, P), "out_s5": (P, 2, 32, N_SEQ)}


def kernel(**inputs):
    import concourse.bacc as bacc
    from concourse.bass_utils import run_bass_kernel_spmd

    nc = bacc.Bacc("TRN2", target_bir_lowering=False, num_devices=1)
    arrays = layout(inputs)
    t = {name: nc.dram_tensor(f"in_{name}", a.shape, F32, kind="ExternalInput").ap() for name, a in arrays.items()}
    t.update({name: nc.dram_tensor(name, shape, F32, kind="ExternalOutput").ap() for name, shape in OUTPUTS.items()})
    build(nc, t)
    r = run_bass_kernel_spmd(nc, [{f"in_{name}": a for name, a in arrays.items()}], core_ids=[0]).results[0]
    r = {name: np.asarray(r[name]) for name in OUTPUTS}

    y = r["out_y"].transpose(2, 1, 0).reshape(T, D_MODEL)
    mem = lambda a: a.transpose(3, 0, 2, 1).reshape(1, 1, N_MEM, 4, HD)
    lru = r["out_lru"].transpose(2, 1, 0).reshape(N_SEQ, W)
    conv = r["out_conv"].transpose(2, 3, 1, 0).reshape(N_SEQ, 3, W)
    s5 = r["out_s5"].transpose(1, 3, 2, 0).reshape(2, N_SEQ, 64, 64)
    gla_s, hg_s = (r[n].transpose(2, 0, 1, 3)[None] for n in ("out_gla_s", "out_hg_s"))
    gla_p, hg_p = r["out_gla_p"][None, None], r["out_hg_p"][None, None]
    result = (y[None, :SEQ], y[SEQ:].reshape(NB, NT, D_MODEL),
              s5[0, None, :1], s5[1, None, :1], hg_p, gla_p, lru[None, :1], conv[None, :1],
              mem(r["out_mem_k"]), mem(r["out_mem_v"]),
              s5[0, None, 1:], s5[1, None, 1:], hg_s, gla_s, lru[None, 1:], conv[None, 1:])
    return tuple(np.ascontiguousarray(a) for a in result)
```

```python
from contextlib import ExitStack

import numpy as np
import concourse.bass as bass
from concourse import mybir

F32 = mybir.dt.float32
F32R = mybir.dt.float32r
ACT = mybir.ActivationFunctionType
ALU = mybir.AluOpType
AX = mybir.AxisListType

P = 128
D_MODEL = 2048
SEQ, NB, NT = 256, 8, 4
TS = NB * NT
T = SEQ + TS
KT = D_MODEL // P
W = D_MODEL // 2
WT = W // P
N_MEM = 256
HD = 256
EPS = 1e-6
CHUNK = 64
LRU_C = 8.0
GLA_RANK = 16
UK = 8
SLOTS = 4
N_SEQ = 1 + NB

STAGES = [("E", 4, 16, 8), ("mE", 4, 12, 4), ("D", 8, 4, 2), ("mD", 4, 12, 4), ("C", 4, 12, 6),
          ("mC", 4, 12, 4), ("B", 8, 8, 4), ("mB", 4, 12, 4), ("A", 8, 4, 2), ("glu", 2, 4, 0),
          ("mA", 4, 12, 4), ("out", 8, 4, 2)]
UNIT0, BLOCK0, UNITS = {}, {}, {}
_u = _b = 0
for _name, _n, _nu, _nb in STAGES:
    UNIT0[_name], BLOCK0[_name], UNITS[_name] = _u, _b, _nu
    _u += _n * _nu
    _b += _n * _nb
N_UNITS = _u
UNIT0["glu"] += 4
N_BLOCKS = {name: nb for name, _, _, nb in STAGES}
HALVES = [64, 32, 16, 8, 4, 2, 1]
LINKS = {"E": 5, "D": 19, "C": 14, "B": 13, "P": 9, "A": 24}
ROUND = 12582912.0
TWO_PI = (6.28125, 0.0019350051879882812, 3.0199159819567e-07)
PI_IN = 3.1415925
DIAG, CROSS, FINAL = 7, 7, 8


class Chain:

    def __init__(self, eng, sem):
        self.eng, self.sem, self.base, self.k, self.i, self.per = eng, sem, 0, 0, None, 0

    def enter(self, i, per):
        self.base, self.k, self.i, self.per = self.base + self.k, 0, i, per

    def leave(self, n):
        assert self.k == self.per, f"a body has {self.k} links, {self.per} said"
        self.base, self.k, self.i = self.base + n * self.per, 0, None

    def link(self, ins):
        ins.then_inc(self.sem, 1)
        self.k += 1
        at = self.base + self.k
        self.eng.wait_ge(self.sem, at if self.i is None else self.i * self.per + at)


def build(nc, t):
    ctx = ExitStack()
    with ctx:
        def sb(name, shape, dt=F32, stack=ctx):
            return stack.enter_context(nc.sbuf_tensor(name, shape, dt))

        sems = {}

        def S(name):
            if name not in sems:
                sems[name] = ctx.enter_context(nc.semaphore(name))
            return sems[name]

        raw = sb("raw", [P, SLOTS, UK, P])
        w_hi = sb("w_hi", [P, SLOTS, UK, P], F32R)
        w_lo = sb("w_lo", [P, SLOTS, UK, P], F32R)
        h_hi = sb("h_hi", [P, KT, T], F32R)
        h_lo = sb("h_lo", [P, KT, T], F32R)
        br_st = ExitStack()
        br_hi = sb("br_hi", [P, WT, T], F32R, br_st)
        br_lo = sb("br_lo", [P, WT, T], F32R, br_st)
        br_st.close()
        spare = sb("spare", [P, WT * T])
        a_P = sb("a_P", [P, 2, 2, 2, T])
        acc = sb("acc", [P, KT, T])
        ident = sb("ident", [P, P])
        ones = sb("ones", [P, P])
        levels = sb("levels", [P, 8, P])
        starts = sb("starts", [P, T])
        chunks = sb("chunks", [P, T])
        in_group = sb("in_group", [P, 8])
        st_group = sb("st_group", [P, 4, 8])
        in_seq = sb("in_seq", [TS, NB])
        norm_cols = sb("norm_cols", [P, 3, KT])
        zero = sb("zero", [P, 1])
        eps = sb("eps", [P, 1])
        half_pi = sb("half_pi", [P, 1])
        rstd = sb("rstd", [P, T])
        sd = sb("sd", [P, T])
        half_out = sb("half_out", [P, T])
        gate_t = sb("gate_t", [P, 2, T])

        e_st = ExitStack()
        m_hi = sb("m_hi", [P, KT, N_MEM], F32R, e_st)
        m_lo = sb("m_lo", [P, KT, N_MEM], F32R, e_st)
        vc = sb("vc", [P, 2, NB, HD], F32, e_st)
        eq = sb("eq", [P, 2, T], F32, e_st)
        e_gate = sb("e_gate", [P, 2, T], F32, e_st)
        e_th = sb("e_th", [P, 2, T], F32, e_st)
        kT = sb("kT", [P, 2, N_MEM], F32, e_st)
        vT = sb("vT", [P, 2, N_MEM], F32, e_st)
        vm = sb("vm", [P, 2, HD], F32, e_st)
        ssc = sb("ssc", [P, 2, TS], F32, e_st)
        prob = sb("prob", [P, 3, N_MEM], F32, e_st)
        mx = sb("mx", [P, 3], F32, e_st)
        rs = sb("rs", [P, 3], F32, e_st)
        pT = sb("pT", [P, 2, T], F32, e_st)
        e_out = sb("e_out", [P, 2, T], F32, e_st)
        e_st.close()
        kc = acc[:].rearrange("p k t -> p (k t)")[:, 0:2 * NB * N_MEM].rearrange(
            "p (d b m) -> p d b m", d=2, b=NB)

        n_st = ExitStack()
        sb("n_pad", [P, 2 * KT * N_MEM], F32R, n_st)
        sq = sb("sq", [P, KT * T], F32, n_st)
        n_st.close()
        o_st = ExitStack()
        x_res = sb("x_res", [P, KT, T], F32, o_st)
        o_sq = sb("o_sq", [P, KT, T], F32, o_st)
        o_st.close()

        d_st = ExitStack()
        d_cols = sb("d_cols", [P, 8, WT], F32, d_st)
        d_sp = sb("d_sp", [P, 8, WT], F32, d_st)
        d_cbuf = sb("d_cbuf", [P, WT, NB, 3], F32, d_st)
        d_h0 = sb("d_h0", [P, WT, NB], F32, d_st)
        d_w = sb("d_w", [P, 2, P], F32, d_st)
        d_xp = sb("d_xp", [P, SEQ + 3], F32, d_st)
        d_xs = sb("d_xs", [P, NB, NT + 3], F32, d_st)
        xc = sb("xc", [P, T], F32, d_st)
        d_r = sb("d_r", [P, T], F32, d_st)
        d_i = sb("d_i", [P, T], F32, d_st)
        d_a = sb("d_a", [P, T], F32, d_st)
        d_L = sb("d_L", [P, T], F32, d_st)
        d_t = sb("d_t", [P, T], F32, d_st)
        d_u = sb("d_u", [P, T], F32, d_st)
        d_gate = sb("d_gate", [P, T], F32, d_st)
        d_th = sb("d_th", [P, T], F32, d_st)
        d_hseq = sb("d_hseq", [P, T], F32, d_st)
        d_out = sb("d_out", [P, T], F32, d_st)
        d_inj = sb("d_inj", [P, NB], F32, d_st)
        d_hlast = sb("d_hlast", [P, WT, N_SEQ], F32, d_st)
        d_clast = sb("d_clast", [P, WT, N_SEQ, 3], F32, d_st)
        d_st.close()

        g_st = ExitStack()
        g_S0 = sb("g_S0", [P, NB, 256], F32, g_st)
        g_X = sb("g_X", [P, 9, T], F32, g_st)
        g_prod = sb("g_prod", [P, 8, P], F32, g_st)
        g_att = sb("g_att", [P, 3, P], F32, g_st)
        g_atts = sb("g_atts", [TS, TS], F32, g_st)
        g_q = sb("g_q", [P, T], F32, g_st)
        g_k = sb("g_k", [P, T], F32, g_st)
        g_g = sb("g_g", [P, T], F32, g_st)
        g_b = sb("g_b", [P, T], F32, g_st)
        g_v = sb("g_v", [P, 2, T], F32, g_st)
        g_vT = sb("g_vT", [P, 3, 256], F32, g_st)
        g_kT = sb("g_kT", [P, 3, P], F32, g_st)
        g_vm = sb("g_vm", [TS, 1024], F32, g_st)
        g_gs = sb("g_gs", [P, 2, T], F32, g_st)
        g_t = sb("g_t", [P, 4, T], F32, g_st)
        g_o2 = sb("g_o2", [P, 2, T], F32, g_st)
        g_Sp = sb("g_Sp", [P, 256], F32, g_st)
        g_eb = sb("g_eb", [P, NB], F32, g_st)
        g_bb = sb("g_bb", [P, 1], F32, g_st)
        g_e = sb("g_e", [P, 2, T], F32, g_st)
        g_o = sb("g_o", [P, 2, T], F32, g_st)
        g_cols = sb("g_cols", [P, 8], F32, g_st)
        g_lb = sb("g_lb", [P, 4, WT], F32, g_st)
        g_wr = sb("g_wr", [P, KT, GLA_RANK], F32, g_st)
        g_r = sb("g_r", [GLA_RANK, T], F32, g_st)
        g_wu = sb("g_wu", [GLA_RANK, P], F32, g_st)
        g_st.close()

        a_st = ExitStack()
        a_p = sb("a_p", [P, 2, 32, 16], F32, a_st)
        a_q = sb("a_q", [P, 2, 32, 16], F32, a_st)
        a_bb = sb("a_bb", [P, 2, WT, 64], F32, a_st)
        a_last = sb("a_last", [P, 2, 32, N_SEQ], F32, a_st)
        a_mag = sb("a_mag", [P, 32], F32, a_st)
        a_inj = a_last[:, :, :, 1:N_SEQ]
        a_d = sb("a_d", [P, WT], F32, a_st)
        a_c = sb("a_c", [P, 2, 32, 16], F32, a_st)
        a_cs = sb("a_cs", [P, 2, 32], F32, a_st)
        a_set_up = ExitStack()
        st_in = sb("st_in", [P, 3, 32], F32, a_set_up)
        ch_in = sb("ch_in", [P, 2, WT, 64], F32, a_set_up)
        ch_dt = sb("ch_dt", [P, WT], F32, a_set_up)[:]
        br_in = sb("br_in", [P, WT, 64], F32, a_set_up)
        bi_in = sb("bi_in", [P, WT, 64], F32, a_set_up)
        h0_in = sb("h0_in", [P, 2, 32, NB], F32, a_set_up)
        st_a, st_th, st_n, st_abs = (sb(f"st_{n}", [P, 32], F32, a_set_up)[:] for n in ("a", "th", "n", "abs"))
        st_tmp = sb("st_tmp", [P, 32, NB], F32, a_set_up)[:]
        ch_a, ch_th, ch_n, ch_mag, ch_sin, ch_cos, ch_abs = (
            sb(f"ch_{n}", [P, WT, 64], F32, a_set_up)[:] for n in ("a", "th", "n", "mag", "sin", "cos", "abs"))
        tab_t1 = sb("tab_t1", [P, 2, 32, 8], F32, a_set_up)
        tab_t2 = sb("tab_t2", [P, 2, 32, 8], F32, a_set_up)
        a_set_up.close()
        st_dt = st_in[:, 2]
        z_hi = sb("z_hi", [P, WT, T], F32R, a_st)
        z_lo = sb("z_lo", [P, WT, T], F32R, a_st)
        zg = sb("zg", [P, WT, T], F32, a_st)
        a_t1 = sb("a_t1", [P, 2, 2, T], F32, a_st)
        a_t2 = sb("a_t2", [P, 2, 2, T], F32, a_st)
        a_m = sb("a_m", [P, 2, 2, T], F32, a_st)
        a_g = sb("a_g", [P, 2, 2, T], F32, a_st)
        a_r = sb("a_r", [P, 2, T], F32, a_st)
        a_B = sb("a_B", [P, 2, 8, 64], F32, a_st)
        rot_1, rot_2 = (spare[:, n * 512:(n + 1) * 512].rearrange("p (k q r) -> p k q r", k=2, q=16) for n in range(2))
        p_tile, q_tile = (spare[:, n * 128:(n + 1) * 128].rearrange("p (k j r) -> p k j r", k=2, j=4) for n in (8, 9))
        a_C = levels[:].rearrange("p (k j) s -> p k j s", k=2)
        a_y, a_ud, a_gs, a_gate, a_th = rstd, half_out, sd, chunks, gate_t[:, 0]
        a_st.close()

        ps = ctx.enter_context(nc.psum_tensor("ps", [P, 8, 512], F32))
        up = ps[:, 5:7].rearrange("p a c -> p (a c)")

        landed = [S(f"landed{s}") for s in range(SLOTS)]
        hi_ready, lo_ready, slots_freed = S("hi_ready"), S("lo_ready"), S("slots_freed")
        bank_free = [S("bank_free0"), S("bank_free1")]
        merge_done = S("merge_done")

        def at(stage, i, u):
            return i * UNITS[stage] + (UNIT0[stage] + u)

        def earlier(stage, i, b):
            return i * (N_BLOCKS[stage] // 2) + (BLOCK0[stage] + b) // 2

        def wait_block(eng, stage, i, b, last_unit):
            eng.wait_ge(slots_freed, at(stage, i, last_unit) + (1 + SLOTS))

        def gates_done(eng, stage, i, half, d):
            eng.wait_ge(slots_freed, at(stage, i, 6 * half + 2 * d + 1) + (1 + SLOTS))

        def wait_taken(eng, stage, i, b):
            eng.wait_ge(bank_free[b % 2], earlier(stage, i, b) + 1)

        def by_seq(ap):
            return ap[:, SEQ:T].rearrange("p (b t) -> p b t", t=NT)

        def heads_before(i, nv):
            return (i, i * 2) if nv == 2 else (i + 4, i + 8)

        block = ctx.enter_context(nc.Block())

        @block.sync
        def _(sp):
            sp.dma_start(acc[:], t["x"]).then_inc(S("x_landed"), 16)

            def load(unit, slot):
                sp.dma_start(raw[:, slot], t["w"][unit].rearrange("p (k c) -> p k c", k=UK)).then_inc(landed[slot], 16)

            for s in range(SLOTS):
                load(s, s)
            sp.wait_ge(S("x_split"), 1)
            sp.dma_start(acc[:, :, 0:N_MEM], t["mem"]).then_inc(S("mem_landed"), 16)
            with sp.Fori(1, N_UNITS // SLOTS) as i:
                for s in range(SLOTS):
                    sp.wait_ge(lo_ready, i * SLOTS + (s - SLOTS + 1))
                    load(i * SLOTS + s, s)

        @block.gpsimd
        def _(pool):
            link = Chain(pool, S("pool_steps")).link

            def load(dst, src, name):
                pool.dma_start(dst, src).then_inc(S(name), 16)

            def tt(op, out, a, b):
                return pool.tensor_tensor(out, a, b, op)

            def ts(out, a, s1, s2, op0, op1=ALU.bypass):
                return pool.tensor_scalar(out, a, s1, s2, op0, op1)

            def wait_before_load(sem, count):
                pool.wait_ge(slots_freed, 1)
                pool.wait_ge(S(sem), count)

            pool.memset(zero[:], 0.0).then_inc(slots_freed, SLOTS)
            load(norm_cols[:], t["norms"], "norms_landed")
            link(pool.memset(ones[:], 1.0))
            link(pool.memset(eps[:], EPS))
            link(pool.memset(half_pi[:], float(np.pi / 2)))
            pool.memset(ident[:], 0.0).then_inc(S("ones_ready"), 1)
            pool.wait_ge(S("ones_ready"), 1)
            link(pool.affine_select(out=ident[:], in_=ident[:], compare_op=ALU.not_equal, fill=1.0,
                                    base=0, pattern=[[-1, P]], channel_multiplier=1))
            for mask, every in ((starts, SEQ), (chunks, CHUNK)):
                link(pool.memset(mask[:], 1.0))
                link(pool.memset(mask[:, 0:SEQ].rearrange("p (c t) -> p c t", t=every)[:, :, 0:1], 0.0))
                link(pool.memset(by_seq(mask)[:, :, 0:1], 0.0))
            link(pool.memset(levels[:], 0.0))
            for l, h in enumerate(HALVES):
                n = P // (2 * h)
                right = levels[:, l, :].rearrange("p (b two h) -> p b two h", two=2, h=h)[:, :, 1, :]
                link(pool.memset(right, 1.0))
                for base, sign in ((0, 1), (h - 1, -1)):
                    link(pool.affine_select(out=right, in_=right, compare_op=ALU.is_ge, fill=0.0, base=base,
                                            pattern=[[-2 * h * sign, n], [0, h]], channel_multiplier=sign))
            link(pool.affine_select(out=levels[:, DIAG, :], in_=levels[:, DIAG, :], compare_op=ALU.not_equal,
                                    fill=1.0, base=0, pattern=[[-1, P]], channel_multiplier=1))
            for mask, width, pattern in ((in_group[:], 16, [[-16, 8]]), (st_group[:], 64, [[128, 4], [-64, 8]]),
                                         (in_seq[:], NT, [[-NT, NB]])):
                link(pool.memset(mask, 1.0))
                for base, sign in ((0, 1), (width - 1, -1)):
                    link(pool.affine_select(out=mask, in_=mask, compare_op=ALU.is_ge, fill=0.0, base=base,
                                            pattern=[[a * sign, b] for a, b in pattern], channel_multiplier=sign))
            pool.memset(zero[:], 0.0).then_inc(S("masks_ready"), 1)

            pool.wait_ge(S("mem_split"), 1)
            with pool.Fori(0, 4) as i:
                wait_before_load("e_scores", i * 3)
                load(kc, t["kc"][i], "kc_landed")
                wait_before_load("e_o", i)
                load(vc[:], t["vc"][i], "vc_landed")
                wait_before_load("bank_free0", earlier("E", i, 4) + 1)
                wait_before_load("bank_free1", earlier("E", i, 5) + 1)
                load(t["out_mem_k"][i], kT[:], "kv_stored")
                load(t["out_mem_v"][i], vT[:], "kv_stored")
            pool.wait_ge(S("kv_stored"), 32 * 4)

            pool.wait_ge(merge_done, 16)
            pool.memset(d_xp[:, 0:3], 0.0).then_inc(S("d_pad"), 1)
            load(d_cols[:], t["d_cols"], "d_params")
            load(d_cbuf[:], t["d_cbuf"], "d_params")
            load(d_h0[:], t["d_h0"], "d_params")
            with pool.Fori(0, WT) as i:
                wait_before_load("d_gates", i)
                load(d_w[:], t["d_w"][i], "d_w_landed")
            pool.wait_ge(S("d_lo"), WT)
            load(t["out_lru"], d_hlast[:], "d_stored")
            load(t["out_conv"], d_clast[:], "d_stored")
            pool.wait_ge(S("d_stored"), 32)

            pool.wait_ge(merge_done, 32)
            load(g_cols[:], t["g_cols"], "g_params")
            load(g_lb[:, 0], t["lb"], "g_params")
            load(g_wr[:], t["w_r"], "g_params")
            with pool.Fori(1, 5) as n:
                i = n - 1
                wait_before_load("c_z", i)
                load(g_wu[:], t["w_up"][i], "c_wu_landed")
                wait_before_load("g_stored", i * 32)
                load(g_S0[:], t["gla"][i], "g_S0_landed")
                wait_before_load("g_new", n)
                load(t["out_gla_s"][i], g_S0[:], "g_stored")
                wait_before_load("g_Sp", n)
                load(t["out_gla_p"][i], g_Sp[:], "g_stored")
            pool.wait_ge(S("g_stored"), 4 * 32)

            pool.wait_ge(merge_done, 48)
            with pool.Fori(5, 13) as n:
                i = n - 5
                wait_before_load("g_stored", i * 32 + 4 * 32)
                load(g_S0[:, :, 0:P], t["hgrn"][i], "g_S0_landed")
                wait_before_load("g_new", n)
                load(t["out_hg_s"][i], g_S0[:, :, 0:P], "g_stored")
                wait_before_load("g_Sp", n)
                load(t["out_hg_p"][i], g_Sp[:, 0:P], "g_stored")
            pool.wait_ge(S("g_stored"), 12 * 32)

            pool.wait_ge(S("g_lo"), 16)
            load(st_in[:], t["a_state"], "a_params")
            load(ch_in[:], t["a_chan"], "a_params")
            load(ch_dt, t["a_chan_dt"], "a_params")
            load(br_in[:], t["a_br"], "a_params")
            load(bi_in[:], t["a_bi"], "a_params")
            load(h0_in[:], t["a_h0"], "a_params")
            load(a_d[:], t["a_d"], "a_params")
            load(a_c[:], t["a_c"], "a_params")
            pool.wait_ge(S("a_params"), 16 * 8)
            pool.wait_ge(S("a_dt"), 2)
            for lr, li, dt, a, th, n, turns in ((st_in[:, 0], st_in[:, 1], st_dt, st_a, st_th, st_n, st_abs),
                                                (ch_in[:, 0], ch_in[:, 1], ch_dt.unsqueeze(2).to_broadcast([P, WT, 64]),
                                                 ch_a, ch_th, ch_n, ch_abs)):
                link(tt(ALU.mult, a, lr, dt))
                link(tt(ALU.mult, th, li, dt))
                link(ts(n, th, float(1 / (2 * np.pi)), ROUND, ALU.mult, ALU.add))
                link(ts(n, n, -ROUND, None, ALU.add))
                for part in TWO_PI:
                    link(ts(turns, n, -part, None, ALU.mult))
                    link(tt(ALU.add, th, th, turns))
                ts(th, th, -PI_IN, PI_IN, ALU.max, ALU.min).then_inc(S("a_theta"), 1)
            pool.wait_ge(S("a_trig"), 8)
            lr, li = ch_in[:, 0], ch_in[:, 1]
            link(tt(ALU.mult, ch_cos, ch_cos, ch_mag))
            link(tt(ALU.mult, ch_sin, ch_sin, ch_mag))
            link(ts(ch_cos, ch_cos, -1.0, None, ALU.add))
            link(tt(ALU.mult, ch_a, lr, lr))
            link(tt(ALU.mult, ch_n, li, li))
            tt(ALU.add, ch_a, ch_a, ch_n).then_inc(S("a_square"), 1)
            pool.wait_ge(S("a_inverse"), 1)
            link(tt(ALU.mult, ch_th, ch_cos, lr))
            link(tt(ALU.mult, ch_n, ch_sin, li))
            link(tt(ALU.add, ch_th, ch_th, ch_n))
            link(tt(ALU.mult, ch_th, ch_th, ch_a))
            link(tt(ALU.mult, ch_abs, ch_sin, lr))
            link(tt(ALU.mult, ch_n, ch_cos, li))
            link(tt(ALU.subtract, ch_abs, ch_abs, ch_n))
            link(tt(ALU.mult, ch_abs, ch_abs, ch_a))
            link(tt(ALU.mult, ch_mag, ch_th, br_in[:]))
            link(tt(ALU.mult, ch_n, ch_abs, bi_in[:]))
            link(tt(ALU.subtract, a_bb[:, 0], ch_mag, ch_n))
            link(tt(ALU.mult, ch_mag, ch_th, bi_in[:]))
            link(tt(ALU.mult, ch_n, ch_abs, br_in[:]))
            link(tt(ALU.add, a_bb[:, 1], ch_mag, ch_n))
            link(tt(ALU.mult, st_a, a_mag[:], a_cs[:, 0]))
            link(tt(ALU.mult, st_n, a_mag[:], a_cs[:, 1]))
            ar, ai = (x.unsqueeze(2).to_broadcast([P, 32, NB]) for x in (st_a, st_n))
            link(tt(ALU.mult, a_inj[:, 0], h0_in[:, 0], ar))
            link(tt(ALU.mult, st_tmp, h0_in[:, 1], ai))
            link(tt(ALU.subtract, a_inj[:, 0], a_inj[:, 0], st_tmp))
            link(tt(ALU.mult, a_inj[:, 1], h0_in[:, 1], ar))
            link(tt(ALU.mult, st_tmp, h0_in[:, 0], ai))
            link(tt(ALU.add, a_inj[:, 1], a_inj[:, 1], st_tmp))
            link(ts(a_c[:, 1], a_c[:, 1], -1.0, None, ALU.mult))
            for table in (a_p, a_q):
                link(pool.memset(table[:, 0, :, 0:1], 1.0))
                link(pool.memset(table[:, 1, :, 0:1], 0.0))
                for m in (1, 2, 4, 8):
                    old = table[:, :, :, 0:m]
                    new = table[:, :, :, m:2 * m]
                    c, s = (a_cs[:, k].unsqueeze(1).unsqueeze(3).to_broadcast([P, 2, 32, m]) for k in range(2))
                    t1, t2 = tab_t1[:, :, :, 0:m], tab_t2[:, :, :, 0:m]
                    link(tt(ALU.mult, t1, old, c))
                    link(tt(ALU.mult, t2, old, s))
                    link(tt(ALU.subtract, new[:, 0], t1[:, 0], t2[:, 1]))
                    link(tt(ALU.add, new[:, 1], t1[:, 1], t2[:, 0]))
                    link(tt(ALU.mult, st_a, a_cs[:, 0], a_cs[:, 0]))
                    link(tt(ALU.mult, st_n, a_cs[:, 1], a_cs[:, 1]))
                    link(tt(ALU.mult, a_cs[:, 1], a_cs[:, 0], a_cs[:, 1]))
                    link(ts(a_cs[:, 1], a_cs[:, 1], 2.0, None, ALU.mult))
                    link(tt(ALU.subtract, a_cs[:, 0], st_a, st_n))
            pool.memset(zero[:], 0.0).then_inc(S("a_set_up"), 1)
            pool.wait_ge(S("a_set_up"), 1)
            pool.memset(zero[:], 0.0).then_inc(S("a_P_used"), 2)

            pool.wait_ge(merge_done, 64)
            pool_ch = Chain(pool, S("a_P_steps"))
            with pool.Fori(0, WT) as i:
                pool_ch.enter(i, LINKS["P"])
                tiles = bass.ds(i * 4, 4)
                pool.tensor_copy(p_tile, a_p[:, :, tiles, :])
                pool_ch.link(pool.tensor_copy(q_tile, a_q[:, :, tiles, :]))
                for pr in range(2):
                    pool.wait_ge(S("a_P_used"), i * 2 + (pr + 1))
                    for j in range(2):
                        n = 2 * pr + j
                        p = p_tile[:, :, n].unsqueeze(2).to_broadcast([P, 2, 16, 16])
                        q = [q_tile[:, k, n].unsqueeze(1).unsqueeze(3).to_broadcast([P, 2, 16, 16]) for k in range(2)]
                        row = lambda k: a_P[:, pr, k, j, 0:SEQ].rearrange("p (q r) -> p q r", q=16)
                        tt(ALU.mult, rot_1, p, q[0])
                        pool_ch.link(tt(ALU.mult, rot_2, p, q[1]))
                        tt(ALU.subtract, row(0), rot_1[:, 0], rot_2[:, 1])
                        pool_ch.link(tt(ALU.add, row(1), rot_1[:, 1], rot_2[:, 0]))
                    for k in range(2):
                        ins = tt(ALU.mult, a_P[:, pr, k, :, SEQ:T].rearrange("p j (b t) -> p j b t", t=NT),
                                 a_P[:, pr, k, :, 0:NT].unsqueeze(2).to_broadcast([P, 2, NB, NT]),
                                 ones[:, 0:2 * TS].rearrange("p (j b t) -> p j b t", j=2, t=NT))
                    ins.then_inc(S("a_P_ready"), 1)
            pool_ch.leave(WT)
            pool.wait_ge(S("a_z_lo"), WT)
            load(t["out_s5"], a_last[:], "a_stored")
            pool.wait_ge(S("a_stored"), 16)

            pool.wait_ge(merge_done, 65)
            load(x_res[:], t["x"], "res_landed")
            for half in range(2):
                ks = slice(half * KT // 2, (half + 1) * KT // 2)
                pool.wait_ge(S("y_ready"), half + 1)
                load(t["out_y"][:, ks], acc[:, ks], "y_stored")
            pool.wait_ge(S("y_stored"), 32)

        @block.scalar
        def _(act):
            def f(out, in_, func, sem, **kw):
                act.activation(out, in_, func, **kw).then_inc(sem if not isinstance(sem, str) else S(sem), 1)

            def split(stage, i, u0, n):
                for u in range(u0, u0 + n):
                    slot = u % SLOTS
                    nth = i * (UNITS[stage] // SLOTS) + ((UNIT0[stage] + u) // SLOTS + 1)
                    act.wait_ge(landed[slot], nth * 16)
                    act.wait_ge(slots_freed, at(stage, i, u) + 1)
                    f(w_hi[:, slot], raw[:, slot], ACT.Copy, hi_ready)

            def time_steps():
                act.wait_ge(S("a_params"), 16 * 8)
                f(st_dt, st_dt, ACT.Exp, "a_dt")
                f(ch_dt, ch_dt, ACT.Exp, "a_dt")

            def decays_and_rotations():
                act.wait_ge(S("a_theta"), 2)
                f(a_mag[:], st_a, ACT.Exp, "a_trig")
                f(a_cs[:, 1], st_th, ACT.Sin, "a_trig")
                f(st_abs, st_th, ACT.Abs, "a_trig")
                f(ch_mag, ch_a, ACT.Exp, "a_trig")
                f(ch_sin, ch_th, ACT.Sin, "a_trig")
                f(ch_abs, ch_th, ACT.Abs, "a_trig")
                act.wait_ge(S("a_trig"), 6)
                f(a_cs[:, 0], st_abs, ACT.Sin, "a_trig", scale=-1.0, bias=half_pi[:])
                f(ch_cos, ch_abs, ACT.Sin, "a_trig", scale=-1.0, bias=half_pi[:])

            def merge(stage, m):
                def pair(i, half, ahead):
                    split(stage, i, 4 + 6 * half, 2)
                    for d in range(2):
                        gates_done(act, stage, i, half, d)
                        act.wait_ge(merge_done, i * 4 + (16 * m + 2 * half))
                        f(gate_t[:, d], ps[:, d, 0:T], ACT.Tanh, bank_free[d], scale=0.5)
                        if ahead:
                            split(stage, i, 6 + 6 * half + 2 * d, 2)

                if stage == "mB":
                    for n in range(2 * 4):
                        pair(n // 2, n % 2, True)
                        if n == 0:
                            time_steps()
                        elif n == 2:
                            decays_and_rotations()
                    return
                with act.Fori(0, 3) as i:
                    pair(i, 0, True)
                    pair(i, 1, True)
                pair(3, 0, True)
                pair(3, 1, stage != "mA")

            def norm(n, x, sq_, pre, landed_at):
                act.wait_ge(S(pre + "_landed"), landed_at)
                f(sq_, x, ACT.Square, pre + "_squared")
                act.wait_ge(S(pre + "_summed"), 1)
                f(sd[:, 0:n], ps[:, 2, 0:n], ACT.Sqrt, pre + "_sd", scale=1.0 / D_MODEL, bias=eps[:])

            act.wait_ge(S("ones_ready"), 1)
            sqv = lambda n: sq[:, 0:KT * n].rearrange("p (k t) -> p k t", k=KT)
            split("E", 0, 0, 4)
            norm(T, acc[:], sqv(T), "x", 16)
            act.wait_ge(S("x_normed"), 1)
            f(h_hi[:], acc[:], ACT.Copy, "h_hi_ready")
            norm(N_MEM, acc[:, :, 0:N_MEM], sqv(N_MEM), "mem", 16)
            act.wait_ge(S("mem_normed"), 1)
            f(m_hi[:], acc[:, :, 0:N_MEM], ACT.Copy, "m_hi_ready")

            with act.Fori(0, 4) as i:
                for b in range(8):
                    if b == 4:
                        act.wait_ge(S("e_scores"), i * 3 + 2)
                        f(ssc[:], ps[:, 4, 0:2 * TS].rearrange("p (a b) -> p a b", a=2), ACT.Copy, "e_ssc")
                    split("E", i, 4 + 2 * b, 2)
                    wait_block(act, "E", i, b, 2 * b + 1)
                    bank = b % 2
                    if 2 <= b < 6:
                        if b == 2:
                            act.wait_ge(S("kv_stored"), i * 32)
                        f((kT if b < 4 else vT)[:, bank], ps[:, bank, 0:N_MEM], ACT.Copy, bank_free[bank])
                    elif b < 2:
                        if b == 0:
                            act.wait_ge(S("e_lo"), i)
                        f(eq[:, bank], ps[:, bank, 0:T], ACT.Copy, bank_free[bank], scale=HD ** -0.5)
                    else:
                        f(e_th[:, bank], ps[:, bank, 0:T], ACT.Tanh, "e_th", scale=0.5)
                    if b == 5:
                        act.wait_ge(S("e_max"), i + 1)
                        for tt in range(2):
                            f(prob[:, tt], ps[:, 3, tt * N_MEM:(tt + 1) * N_MEM], ACT.Exp, "e_exp",
                              bias=mx[:, tt:tt + 1], accum_out=rs[:, tt:tt + 1])
                        f(prob[0:TS, 2], ps[0:TS, 5, 0:N_MEM], ACT.Exp, "e_exp",
                          bias=mx[0:TS, 2:3], accum_out=rs[0:TS, 2:3])
                        act.wait_ge(S("e_vt"), i + 1)
                        f(vm[:], ps[:, 6].rearrange("p (a b) -> p a b", a=2), ACT.Copy, "e_vm")
                act.wait_ge(S("e_pt"), i + 1)
                f(pT[:, :, 0:SEQ], ps[:, 2].rearrange("p (a t) -> p a t", a=2), ACT.Copy, "e_pT")
                f(pT[:, :, SEQ:T], ps[:, 4, 0:2 * TS].rearrange("p (a t) -> p a t", a=2), ACT.Copy, "e_pT")
                act.wait_ge(S("e_out"), i + 1)
                f(br_hi[:, bass.ds(i * 2, 2), :], e_out[:], ACT.Copy, "e_hi", scale=0.5)
            merge("mE", 0)

            act.wait_ge(merge_done, 16)
            act.wait_ge(S("d_abs_lam"), 1)
            f(d_sp[:, 0], d_sp[:, 1], ACT.Exp, "d_exp_lam", scale=-1.0)
            act.wait_ge(S("d_pad"), 1)
            with act.Fori(0, WT) as i:
                wait_block(act, "D", i, 0, 1)
                f(d_xp[:, 3:3 + SEQ], ps[:, 0, 0:SEQ], ACT.Copy, "d_xp")
                f(d_xs[:, :, 3:3 + NT], ps[:, 0, SEQ:T].rearrange("p (b t) -> p b t", t=NT), ACT.Copy, bank_free[0])
                split("D", i, 4, 2)
                wait_block(act, "D", i, 1, 3)
                f(d_th[:], ps[:, 1, 0:T], ACT.Tanh, "d_th", scale=0.5)
                split("D", i, 6, 2)
                act.wait_ge(S("d_gates"), i + 1)
                act.wait_ge(S("d_halved"), 1)
                f(d_r[:], ps[:, 2, 0:T], ACT.Tanh, "d_r", scale=0.5, bias=d_sp[:, 5, bass.ds(i, 1)])
                f(d_i[:], ps[:, 3, 0:T], ACT.Tanh, "d_i", scale=0.5, bias=d_sp[:, 6, bass.ds(i, 1)])
                act.wait_ge(S("d_L"), i + 1)
                f(d_a[:], d_L[:], ACT.Exp, "d_a")
                f(d_t[:], d_L[:], ACT.Tanh, "d_t", scale=-1.0)
                act.wait_ge(S("d_s"), i + 1)
                f(d_u[:], d_t[:], ACT.Sqrt, "d_sqrt")
                act.wait_ge(S("d_out"), i + 1)
                f(br_hi[:, bass.ds(i, 1), :], d_out[:].unsqueeze(1), ACT.Copy, "d_hi", scale=0.5)
            merge("mD", 1)

            def waits(i, nv):
                heads, v0 = heads_before(i, nv)

                def w(name, per=1, k=1):
                    act.wait_ge(S("g_" + name), heads * per + k)

                def wv(name, k):
                    act.wait_ge(S("g_" + name), v0 + k)

                return w, wv

            def split_values(i, nv):
                w, _ = waits(i, nv)
                w("vt")
                for tt in range(2):
                    f(g_vT[:, tt, 0:nv * P], ps[:, 2 + tt, 0:nv * P], ACT.Copy, "g_vT")
                f(g_vT[0:TS, 2, 0:nv * P], ps[0:TS, 4, 0:nv * P], ACT.Copy, "g_vT")

            def distances(i, nv):
                w, _ = waits(i, nv)
                w("D")
                f(g_X[:, 0:5, 0:SEQ], g_X[:, 0:5, 0:SEQ], ACT.Exp, "g_E")
                f(g_X[:, 5:9, :], g_X[:, 5:9, :], ACT.Exp, "g_E")
                w("new", 1, 0)
                f(g_eb[:], by_seq(g_b)[:, :, NT - 1], ACT.Exp, "g_E")

            def mix(i, nv):
                w, wv = waits(i, nv)
                w("kt")
                f(g_kT[:, 0:2], ps[:, 5, 0:2 * P].rearrange("p (a b) -> p a b", a=2), ACT.Copy, "g_kT")
                f(g_kT[0:TS, 2], ps[0:TS, 5, 2 * P:3 * P], ACT.Copy, "g_kT")
                f(g_att[:, 1], ps[:, 6, 0:P], ACT.Copy, "g_cross_out")
                w("o")
                for v in range(nv):
                    f(g_o2[:, v], ps[:, 2 + v, 0:T], ACT.Square, "g_sq")
                w("Sp_raw")
                w("stored", 32, 0)
                f(g_Sp[:, 0:nv * P], ps[:, 4, 0:nv * P], ACT.Copy, "g_Sp")
                w("ssq")
                f(g_t[:, 2], ps[:, 7, 0:T], ACT.Ln, "g_ln_ms", scale=1.0 / (nv * P), bias=eps[:])
                w("ln_ms")
                f(g_t[:, 3], g_t[:, 2], ACT.Exp, "g_rstd", scale=-0.5)
                for v in range(nv):
                    wv("out", v + 1)
                    f(br_hi[:, bass.ds(i * nv + v, 1), :], g_o[:, v:v + 1], ACT.Copy, "g_hi")

            act.wait_ge(merge_done, 32)
            act.wait_ge(S("c_rT_raw"), 1)
            f(g_r[:], ps[0:GLA_RANK, 2, 0:T], ACT.Copy, "c_rT")
            act.wait_ge(S("lb_shift"), 1)
            f(g_lb[:, 2], g_lb[:, 1], ACT.Exp, "lb_exp")
            with act.Fori(0, 4) as i:
                for b in range(6):
                    if b == 4:
                        split_values(i, 2)
                        distances(i, 2)
                    split("C", i, 4 + 2 * b, 2)
                    wait_block(act, "C", i, b, 2 * b + 1)
                    src = ps[:, b % 2, 0:T]
                    if b == 0:
                        f(g_q[:], src, ACT.Copy, bank_free[0], scale=P ** -0.5)
                    elif b == 1:
                        f(g_k[:], src, ACT.Copy, bank_free[1])
                        act.wait_ge(S("c_z"), i + 1)
                        bias = g_cols[:, bass.ds(i + 4, 1)]
                        f(g_t[:, 0], ps[:, 7, 0:T], ACT.Abs, "c_abs", bias=bias)
                        f(g_t[:, 2], ps[:, 7, 0:T], ACT.Identity, "c_zb", bias=bias)
                        act.wait_ge(S("c_abs"), i + 1)
                        f(g_t[:, 1], g_t[:, 0], ACT.Exp, "c_w", scale=-1.0)
                        act.wait_ge(S("c_w"), i + 1)
                        f(g_t[:, 3], g_t[:, 1], ACT.Ln, "c_l1", bias=1.0)
                    elif b < 4:
                        f(g_v[:, b - 2], src, ACT.Copy, bank_free[b % 2])
                    else:
                        f(g_e[:, b - 4], src, ACT.Exp, "g_ge", scale=-1.0)
                mix(i, 2)
            merge("mC", 2)

            act.wait_ge(merge_done, 48)
            with act.Fori(0, 8) as i:
                for b in range(4):
                    split("B", i, 4 + 2 * b, 2)
                    wait_block(act, "B", i, b, 2 * b + 1)
                    src = ps[:, b % 2, 0:T]
                    if b == 0:
                        f(g_t[:, 2], src, ACT.Copy, "b_zb")
                        f(g_t[:, 0], src, ACT.Abs, bank_free[0])
                        wait_taken(act, "B", i, 0)
                        f(g_t[:, 1], g_t[:, 0], ACT.Exp, "b_w", scale=-1.0)
                        act.wait_ge(S("b_w"), i + 1)
                        f(g_t[:, 3], g_t[:, 1], ACT.Ln, "b_l1", bias=1.0)
                    elif b == 1:
                        f(g_q[:], src, ACT.Copy, bank_free[1])
                        act.wait_ge(S("b_kz"), i + 1)
                        f(g_k[:], g_k[:], ACT.Exp, "b_kexp")
                        f(g_t[:, 1], g_t[:, 0], ACT.Exp, "b_em")
                        act.wait_ge(S("b_mixed"), i + 1)
                        f(g_t[:, 3], g_t[:, 1], ACT.Ln, "b_ln")
                    elif b == 2:
                        f(g_v[:, 0], src, ACT.Copy, bank_free[0])
                    else:
                        f(g_e[:, 0], src, ACT.Exp, "g_ge", scale=-1.0)
                split_values(i, 1)
                distances(i, 1)
                mix(i, 1)
            merge("mB", 3)

            act.wait_ge(merge_done, 64)
            act.wait_ge(S("a_set_up"), 1)
            with act.Fori(0, WT) as i:
                split("A", i, 4, 2)
                wait_block(act, "A", i, 0, 1)
                f(a_ud[:], ps[:, 0, 0:T], ACT.Copy, bank_free[0])
                split("A", i, 6, 2)
                wait_block(act, "A", i, 1, 3)
                act.wait_ge(S("a_z_lo"), i)
                f(a_th, ps[:, 1, 0:T], ACT.Tanh, "a_gate_th", scale=0.5)
                for pr in range(2):
                    act.wait_ge(S("a_scanned"), i * 4 + 2 * pr)
                    for j in range(2):
                        f(a_r[:, j], starts[:], ACT.Copy, "a_r", scale=a_mag[:, bass.ds(i * 4 + (2 * pr + j), 1)])
                act.wait_ge(S("a_inner"), i + 1)
                f(a_th, a_gs[:], ACT.Tanh, "a_tanh", scale=float(np.sqrt(2 / np.pi)))
                act.wait_ge(S("a_z2"), i + 1)
                f(z_hi[:, bass.ds(i, 1), :], a_th.unsqueeze(1), ACT.Copy, "a_z_hi", scale=0.5)
            with act.Fori(0, 2) as i:
                split("glu", i, 0, 4)
                for b in range(4):
                    wait_block(act, "glu", i, b, b)
                    act.wait_ge(S("glu_lo"), i * 4 + b)
                    f(a_th, ps[:, 2 + b % 2, 0:T], ACT.Tanh, "glu_th", scale=0.5)
                    act.wait_ge(S("glu_out"), i * 4 + (b + 1))
                    f(br_hi[:, bass.ds(i * 4 + b, 1), :], a_y[:].unsqueeze(1), ACT.Copy, "glu_hi", scale=0.125)
            merge("mA", 4)

            act.wait_ge(merge_done, 80)
            f(h_hi[:], acc[:], ACT.Copy, "o_hi_ready")
            split("out", 0, 0, 4)
            act.wait_ge(S("o_split"), 1)

            def out_blocks(i, ahead):
                for b in range(2):
                    wait_block(act, "out", i, b, 2 * b + 1)
                    f(acc[:, bass.ds(i * 2 + b, 1), :], ps[:, b, 0:T].unsqueeze(1), ACT.Copy, "o_copied")
                    f(o_sq[:, bass.ds(i * 2 + b, 1), :], ps[:, b, 0:T].unsqueeze(1), ACT.Square, bank_free[b])
                    if ahead:
                        split("out", i, 4 + 2 * b, 2)

            with act.Fori(0, 7) as i:
                out_blocks(i, True)
            out_blocks(7, False)
            act.wait_ge(S("res_summed"), 1)
            f(sd[:], ps[:, 2, 0:T], ACT.Sqrt, "res_sd", scale=1.0 / D_MODEL, bias=eps[:])

        @block.vector
        def _(dve):
            ch = Chain(dve, S("dve_steps"))
            link = ch.link

            def sg(ins, name):
                ins.then_inc(S(name) if isinstance(name, str) else name, 1)

            def mul(out, a, b):
                return dve.tensor_tensor(out, a, b, ALU.mult)

            def add(out, a, b):
                return dve.tensor_tensor(out, a, b, ALU.add)

            def sub(out, a, b):
                return dve.tensor_tensor(out, a, b, ALU.subtract)

            def ts(out, a, s1, s2, op0, op1=ALU.bypass):
                return dve.tensor_scalar(out, a, s1, s2, op0, op1)

            def stt(out, a, s, b, op0, op1):
                return dve.scalar_tensor_tensor(out=out, in0=a, scalar=s, in1=b, op0=op0, op1=op1)

            def split(stage, i, u0, n):
                for u in range(u0, u0 + n):
                    slot = u % SLOTS
                    dve.wait_ge(hi_ready, at(stage, i, u) + 1)
                    sg(sub(w_lo[:, slot], raw[:, slot], w_hi[:, slot].bitcast(F32)), lo_ready)

            def low(dst, src, scale, high):
                return stt(dst, src, scale, high.bitcast(F32), ALU.mult, ALU.subtract)

            def merge(stage, m):
                def pair(i, half, ahead):
                    split(stage, i, 4 + 6 * half, 2)
                    for d in range(2):
                        if ahead:
                            split(stage, i, 6 + 6 * half + 2 * d, 2)
                        nth = 2 * half + d
                        dve.wait_ge(slots_freed, at(stage, i, 4 + 6 * half + d) + (1 + SLOTS))
                        wait_taken(dve, stage, i, nth)
                        sg(stt(half_out[:], gate_t[:, d], 1.0, ps[:, 2 + d, 0:T], ALU.add, ALU.mult), "weighed")
                        dve.wait_ge(S("weighed"), i * 4 + (16 * m + nth + 1))
                        dst, src = acc[:, bass.ds(i * 4 + nth, 1), :], half_out[:].unsqueeze(1)
                        if m == 0:
                            ins = ts(dst, src, 0.5, None, ALU.mult)
                        else:
                            ins = stt(dst, src, 0.5, dst, ALU.mult, ALU.add)
                        sg(ins, merge_done)
                        dve.wait_ge(merge_done, i * 4 + (16 * m + nth + 1))

                if stage == "mB":
                    for n in range(2 * 4):
                        pair(n // 2, n % 2, True)
                        if n == 4:
                            dve.wait_ge(S("a_square"), 1)
                            sg(dve.reciprocal(ch_a, ch_a), "a_inverse")
                    return
                with dve.Fori(0, 3) as i:
                    pair(i, 0, True)
                    pair(i, 1, True)
                pair(3, 0, True)
                pair(3, 1, stage != "mA")

            def norm(n, x, sq_, pre, gains):
                dve.wait_ge(S(pre + "_squared"), 1)
                sg(dve.tensor_reduce(half_out[:, 0:n], sq_.rearrange("p k t -> p t k"), AX.X, ALU.add), pre + "_ksum")
                dve.wait_ge(S(pre + "_sd"), 1)
                link(dve.reciprocal(rstd[:, 0:n], sd[:, 0:n]))
                link(mul(x, x, rstd[:, 0:n].unsqueeze(1).to_broadcast([P, KT, n])))
                dve.wait_ge(S("norms_landed"), 16)
                return mul(x, x, norm_cols[:, gains, :].unsqueeze(2).to_broadcast([P, KT, n]))

            sqv = lambda n: sq[:, 0:KT * n].rearrange("p (k t) -> p k t", k=KT)
            split("E", 0, 0, 4)
            sg(norm(T, acc[:], sqv(T), "x", 0), "x_normed")
            dve.wait_ge(S("h_hi_ready"), 1)
            sg(sub(h_lo[:], acc[:], h_hi[:].bitcast(F32)), "x_split")
            sg(norm(N_MEM, acc[:, :, 0:N_MEM], sqv(N_MEM), "mem", 2), "mem_normed")
            dve.wait_ge(S("m_hi_ready"), 1)
            sg(sub(m_lo[:], acc[:, :, 0:N_MEM], m_hi[:].bitcast(F32)), "mem_split")

            with dve.Fori(0, 4) as i:
                ch.enter(i, LINKS["E"])
                split("E", i, 4, 10)
                dve.wait_ge(S("e_scores"), i * 3 + 3)
                link(dve.tensor_reduce(mx[:, 0:2], ps[:, 3].rearrange("p (a m) -> p a m", a=2), AX.X, ALU.max))
                link(dve.tensor_reduce(mx[0:TS, 2:3], ps[0:TS, 5, 0:N_MEM], AX.X, ALU.max))
                link(ts(mx[:, 0:2], mx[:, 0:2], -1.0, None, ALU.mult))
                sg(ts(mx[0:TS, 2:3], mx[0:TS, 2:3], -1.0, None, ALU.mult), "e_max")
                split("E", i, 14, 2)
                dve.wait_ge(S("e_exp"), i * 3 + 3)
                link(dve.reciprocal(rs[:, 0:2], rs[:, 0:2]))
                link(dve.reciprocal(rs[0:TS, 2:3], rs[0:TS, 2:3]))
                for tt in range(2):
                    sg(ts(prob[:, tt], prob[:, tt], rs[:, tt:tt + 1], None, ALU.mult), "e_prob")
                sg(ts(prob[0:TS, 2], prob[0:TS, 2], rs[0:TS, 2:3], None, ALU.mult), "e_prob")
                for b in range(2):
                    split("E", i, 16 + 2 * b, 2)
                    dve.wait_ge(S("e_th"), i * 2 + (b + 1))
                    sg(stt(e_gate[:, b], e_th[:, b], 1.0, ps[:, b, 0:T], ALU.add, ALU.mult), bank_free[b])
                dve.wait_ge(S("e_o"), i + 1)
                wait_taken(dve, "E", i, 6)
                wait_taken(dve, "E", i, 7)
                sg(mul(e_out[:], ps[:, 6:8, 0:T], e_gate[:]), "e_out")
                dve.wait_ge(S("e_hi"), i + 1)
                dve.wait_ge(S("e_out"), i + 1)
                sg(low(br_lo[:, bass.ds(i * 2, 2), :], e_out[:], 0.5, br_hi[:, bass.ds(i * 2, 2), :]), "e_lo")
            ch.leave(4)
            merge("mE", 0)

            dve.wait_ge(S("d_params"), 48)
            lam = d_cols[:, 7]
            link(ts(d_sp[:, 2], lam, -1.0, 0.0, ALU.mult, ALU.max))
            link(ts(d_sp[:, 3], lam, 0.0, None, ALU.max))
            sg(add(d_sp[:, 1], d_sp[:, 2], d_sp[:, 3]), "d_abs_lam")
            sg(ts(d_sp[:, 5:7], d_cols[:, 5:7], 0.5, None, ALU.mult), "d_halved")
            dve.wait_ge(S("d_exp_lam"), 1)
            y, z, z2, poly = d_sp[:, 0], d_sp[:, 1], d_sp[:, 3], d_sp[:, 4]
            link(ts(z, y, 2.0, None, ALU.add))
            link(dve.reciprocal(z, z))
            link(mul(z, z, y))
            link(mul(z2, z, z))
            link(ts(poly, z2, 1.0 / 17, 1.0 / 15, ALU.mult, ALU.add))
            for odd in (13, 11, 9, 7, 5, 3, 1):
                link(mul(poly, poly, z2))
                link(ts(poly, poly, 1.0 / odd, None, ALU.add))
            link(mul(poly, poly, z))
            link(stt(poly, poly, 2.0, d_sp[:, 2], ALU.mult, ALU.add))
            link(ts(d_sp[:, 7], poly, -LRU_C / 2, None, ALU.mult))
            with dve.Fori(0, WT) as i:
                ch.enter(i, LINKS["D"])
                split("D", i, 4, 2)
                wait_taken(dve, "D", i, 0)
                link(dve.tensor_copy(d_xs[:, :, 0:3], d_cbuf[:, bass.ds(i, 1)].rearrange("p a b c -> p (a b) c")))
                xp, xs = xc[:, 0:SEQ], by_seq(xc)
                for j in range(4):
                    w = d_cols[:, j, bass.ds(i, 1)]
                    if j == 0:
                        bias = d_cols[:, 4, bass.ds(i, 1)]
                        link(ts(xp, d_xp[:, 0:SEQ], w, bias, ALU.mult, ALU.add))
                        link(ts(xs, d_xs[:, :, 0:NT], w, bias, ALU.mult, ALU.add))
                    else:
                        link(stt(xp, d_xp[:, j:j + SEQ], w, xp, ALU.mult, ALU.add))
                        ins = stt(xs, d_xs[:, :, j:j + NT], w, xs, ALU.mult, ALU.add)
                        link(ins) if j < 3 else sg(ins, "d_xc")
                link(dve.tensor_copy(d_clast[:, bass.ds(i, 1), 0:1, :].rearrange("p a b c -> p (a b) c"),
                                     d_xp[:, SEQ:SEQ + 3].unsqueeze(1)))
                link(dve.tensor_copy(d_clast[:, bass.ds(i, 1), 1:N_SEQ, :].rearrange("p a b c -> p (a b) c"),
                                     d_xs[:, :, NT:NT + 3]))
                split("D", i, 6, 2)
                dve.wait_ge(S("d_th"), i + 1)
                sg(stt(d_gate[:], d_th[:], 1.0, ps[:, 1, 0:T], ALU.add, ALU.mult), bank_free[1])
                dve.wait_ge(S("d_r"), i + 1)
                sg(ts(d_L[:], d_r[:], 1.0, d_sp[:, 7, bass.ds(i, 1)], ALU.add, ALU.mult), "d_L")
                dve.wait_ge(S("d_i"), i + 1)
                link(stt(d_i[:], d_i[:], 1.0, xc[:], ALU.add, ALU.mult))
                dve.wait_ge(S("d_a"), i + 1)
                link(mul(d_r[:], d_a[:], d_a[:]))
                dve.wait_ge(S("d_t"), i + 1)
                sg(stt(d_t[:], d_r[:], 1.0, d_t[:], ALU.add, ALU.mult), "d_s")
                dve.wait_ge(S("d_sqrt"), i + 1)
                link(stt(d_u[:], d_i[:], 0.5, d_u[:], ALU.mult, ALU.mult))
                link(mul(d_inj[:], by_seq(d_a)[:, :, 0], d_h0[:, bass.ds(i, 1)].rearrange("p a b -> p (a b)")))
                link(add(by_seq(d_u)[:, :, 0], by_seq(d_u)[:, :, 0], d_inj[:]))
                link(mul(d_a[:], d_a[:], starts[:]))
                link(dve.tensor_tensor_scan(d_hseq[:], d_a[:], d_u[:], 0.0, ALU.mult, ALU.add))
                link(dve.tensor_copy(d_hlast[:, bass.ds(i, 1), 0:1], d_hseq[:, SEQ - 1:SEQ].unsqueeze(1)))
                link(dve.tensor_copy(d_hlast[:, bass.ds(i, 1), 1:N_SEQ], by_seq(d_hseq)[:, :, NT - 1].unsqueeze(1)))
                sg(mul(d_out[:], d_hseq[:], d_gate[:]), "d_out")
                dve.wait_ge(S("d_hi"), i + 1)
                dve.wait_ge(S("d_out"), i + 1)
                sg(low(br_lo[:, bass.ds(i, 1), :], d_out[:].unsqueeze(1), 0.5, br_hi[:, bass.ds(i, 1), :]), "d_lo")
            ch.leave(WT)
            merge("mD", 1)

            def silu(nth, v, bank):
                dve.wait_ge(S("g_ge"), nth)
                e = g_e[:, v]
                link(ts(e, e, 1.0, None, ALU.add))
                link(dve.reciprocal(e, e))
                sg(mul(g_gs[:, v], e, ps[:, bank, 0:T]), bank_free[bank])

            def halves(ap, h):
                n = T if 2 * h <= NT else SEQ
                return ap[:, 0:n].rearrange("p (b two h) -> p b two h", two=2, h=h), n // (2 * h)

            def mix(stage, i, nv):
                heads, v0 = heads_before(i, nv)

                def w(name, per=1, k=1):
                    dve.wait_ge(S("g_" + name), heads * per + k)

                def wv(name, k):
                    dve.wait_ge(S("g_" + name), v0 + k)

                link(dve.tensor_tensor_scan(g_b[:], chunks[:], g_g[:], 0.0, ALU.mult, ALU.add))
                for l, h in enumerate(HALVES):
                    (bv, n), (xv, _) = halves(g_b, h), halves(g_X[:, l], h)
                    mid = bv[:, :, 0, h - 1:h].to_broadcast([P, n, h])
                    if h == CHUNK:
                        dve.tensor_copy(xv[:, :, 1], bv[:, :, 1])
                    else:
                        sub(xv[:, :, 1], bv[:, :, 1], mid)
                    sub(xv[:, :, 0], mid, bv[:, :, 0])
                c = lambda n: slice(n * CHUNK, (n + 1) * CHUNK)
                last = lambda n: g_b[:, (n + 1) * CHUNK - 1:(n + 1) * CHUNK]
                cross, final = g_X[:, CROSS], g_X[:, FINAL]
                dve.tensor_copy(cross[:, c(2)], g_b[:, c(2)])
                ts(cross[:, c(3)], g_b[:, c(3)], last(2), None, ALU.add)
                dve.tensor_copy(cross[:, SEQ:T], g_b[:, SEQ:T])
                ts(cross[:, c(1)], g_b[:, c(1)], last(1), -1.0, ALU.subtract, ALU.mult)
                ts(final[:, c(2)], g_b[:, c(2)], last(2), -1.0, ALU.subtract, ALU.mult)
                ts(final[:, c(3)], g_b[:, c(3)], last(3), -1.0, ALU.subtract, ALU.mult)
                sub(by_seq(final), by_seq(g_b)[:, :, NT - 1:NT].to_broadcast([P, NB, NT]), by_seq(g_b))
                link(add(g_bb[:], last(2), last(3)))
                link(ts(cross[:, c(0)], g_X[:, 0, c(0)], last(1), None, ALU.add))
                ts(final[:, c(2)], final[:, c(2)], last(3), None, ALU.add)
                sg(ts(final[:, 0:2 * CHUNK], cross[:, 0:2 * CHUNK], g_bb[:], None, ALU.add), "g_D")
                split(stage, i, 8, 4)
                w("E", 3, 3)
                for l, h in enumerate(HALVES):
                    (xv, _), (qv, _), (kv, _) = halves(g_X[:, l], h), halves(g_q, h), halves(g_k, h)
                    mul(xv[:, :, 1], xv[:, :, 1], qv[:, :, 1])
                    mul(xv[:, :, 0], xv[:, :, 0], kv[:, :, 0])
                mul(cross[:, 0:P], cross[:, 0:P], g_k[:, 0:P])
                mul(cross[:, P:T], cross[:, P:T], g_q[:, P:T])
                sg(mul(final, final, g_k[:]), "g_X")
                if nv == 2:
                    split(stage, i, 12, 2)
                for v in range(nv):
                    silu(v0 + (v + 1), v, v if nv == 2 else 1)
                if nv == 2:
                    split(stage, i, 14, 2)
                for n in range(2):
                    w("levels", 3, 1 + 2 * n)
                    link(mul(g_prod[:].rearrange("p l t -> p (l t)"), ps[:, 2:4].rearrange("p a t -> p (a t)"),
                             levels[:].rearrange("p l t -> p (l t)")))
                    sg(dve.tensor_reduce(g_att[:, 2 * n], g_prod[:].rearrange("p l t -> p t l"), AX.X, ALU.add), "g_att")
                    w("att", 3, 1 + 2 * n)
                    if n == 0:
                        w("levels", 3, 2)
                        own = g_prod[0:TS, 0:3, 0:TS]
                        link(mul(own, ps[0:TS, 4, 0:3 * TS].rearrange("p (l t) -> p l t", t=TS), levels[0:TS, 5:8, 0:TS]))
                        sg(dve.tensor_reduce(g_atts[:], own.rearrange("p l t -> p t l"), AX.X, ALU.add), "g_att")
                        w("att", 3, 2)

                def new_states(half):
                    n = NB // nv
                    wv("up", half + 1)
                    if half == 0:
                        w("o")
                    for b in range(n):
                        s = g_S0[:, half * n + b, 0:nv * P]
                        ins = stt(s, s, g_eb[:, half * n + b:half * n + b + 1], up[:, b * nv * P:(b + 1) * nv * P],
                                  ALU.mult, ALU.add)
                    sg(ins, "g_new" if half == nv - 1 else "g_half_new")

                def own_values(half):
                    n = NB // nv
                    if half:
                        wv("up", half)
                    sg(mul(g_vm[:].rearrange("p (b v) -> p b v", v=nv * P),
                           g_vT[0:TS, 2, 0:nv * P].unsqueeze(1).to_broadcast([TS, n, nv * P]),
                           in_seq[:, half * n:(half + 1) * n].unsqueeze(2).to_broadcast([TS, n, nv * P])), "g_vm")

                w("vT", 3, 3)
                own_values(0)
                new_states(0)
                if nv == 2:
                    own_values(1)
                w("rstd")
                for v in range(nv):
                    link(mul(g_o[:, v], ps[:, 2 + v, 0:T], g_t[:, 3]))
                    gain = g_cols[:, v:v + 1] if nv == 2 else g_cols[:, 2:3]
                    sg(stt(g_o[:, v], g_o[:, v], gain, g_gs[:, v], ALU.mult, ALU.mult), "g_out")
                if nv == 2:
                    new_states(1)
                for v in range(nv):
                    wv("out", v + 1)
                    wv("hi", v + 1)
                    sg(low(br_lo[:, bass.ds(i * nv + v, 1), :], g_o[:, v:v + 1], 1.0,
                           br_hi[:, bass.ds(i * nv + v, 1), :]), "g_lo")

            dve.wait_ge(S("g_params"), 48)
            sg(sub(g_lb[:, 1], g_lb[:, 0], g_lb[:, 0]), "lb_shift")
            dve.wait_ge(S("lb_exp"), 1)
            link(dve.reciprocal(g_lb[:, 3], g_lb[:, 2]))
            link(mul(g_lb[:, 3], g_lb[:, 3], g_lb[:, 2]))
            link(sub(g_lb[:, 0], g_lb[:, 3], g_lb[:, 3]))
            link(ts(g_lb[:, 1], g_lb[:, 0], -1.0, 1.0, ALU.mult, ALU.add))
            with dve.Fori(0, 4) as i:
                ch.enter(i, LINKS["C"])
                split("C", i, 4, 4)
                dve.wait_ge(S("c_l1"), i + 1)
                link(stt(g_g[:], g_t[:, 2], 0.0, g_t[:, 3], ALU.min, ALU.subtract))
                link(ts(g_g[:], g_g[:], 1.0 / 16.0, None, ALU.mult))
                mix("C", i, 2)
            ch.leave(4)
            merge("mC", 2)

            with dve.Fori(0, 8) as i:
                ch.enter(i, LINKS["B"])
                split("B", i, 4, 4)
                dve.wait_ge(S("b_l1"), i + 1)
                link(stt(g_g[:], g_t[:, 2], 0.0, g_t[:, 3], ALU.min, ALU.subtract))
                link(sub(g_k[:], g_g[:], g_t[:, 2]))
                sg(ts(g_t[:, 0], g_g[:], -1.0, 40.0, ALU.mult, ALU.min), "b_kz")
                bound, rest = g_lb[:, 0, bass.ds(i, 1)], g_lb[:, 1, bass.ds(i, 1)]
                dve.wait_ge(S("b_em"), i + 1)
                sg(ts(g_t[:, 1], g_t[:, 1], bound, rest, ALU.mult, ALU.add), "b_mixed")
                link(ts(g_k[:], g_k[:], rest, None, ALU.mult))
                dve.wait_ge(S("b_ln"), i + 1)
                link(add(g_g[:], g_g[:], g_t[:, 3]))
                mix("B", i, 1)
            ch.leave(8)
            merge("mB", 3)

            dve.wait_ge(S("a_set_up"), 1)
            with dve.Fori(0, WT) as i:
                ch.enter(i, LINKS["A"])
                for k in range(2):
                    sg(mul(a_B[:, k], a_bb[:, k, bass.ds(i, 1), :].to_broadcast([P, 8, 64]),
                           in_group[:].unsqueeze(2).to_broadcast([P, 8, 64])), "a_B")
                for k in range(2):
                    sg(mul(a_C[:, k].rearrange("p j (g o) -> p j g o", g=8),
                           a_c[:, k, bass.ds(i * 4, 4), :].unsqueeze(2).to_broadcast([P, 4, 8, 16]),
                           st_group[:].unsqueeze(3).to_broadcast([P, 4, 8, 16])), "a_C")
                split("A", i, 4, 4)
                dve.wait_ge(S("a_gate_th"), i + 1)
                sg(stt(a_gate[:], a_th, 1.0, ps[:, 1, 0:T], ALU.add, ALU.mult), bank_free[1])
                for pr in range(2):
                    cos, sin = (a_P[:, pr, k].unsqueeze(1).to_broadcast([P, 2, 2, T]) for k in range(2))
                    dve.wait_ge(S("a_P_ready"), i * 2 + (pr + 1))
                    dve.wait_ge(S("a_x"), i * 2 + (pr + 1))
                    x = ps[:, 2:6, 0:T].rearrange("p (k j) t -> p k j t", k=2)
                    link(mul(a_t1[:], x, cos))
                    sg(mul(a_t2[:], x, sin), "a_x_used")
                    dve.wait_ge(S("a_x_used"), i * 2 + (pr + 1))
                    dve.wait_ge(S("a_y_part"), i * 2 + pr)
                    link(add(a_m[:, 0], a_t1[:, 0], a_t2[:, 1]))
                    link(sub(a_m[:, 1], a_t1[:, 1], a_t2[:, 0]))
                    for k in range(2):
                        first = a_m[:, k, :, SEQ:T].rearrange("p j (b t) -> p j b t", t=NT)[:, :, :, 0]
                        link(add(first, first, a_inj[:, k, bass.ds(i * 4 + 2 * pr, 2), :]))
                    dve.wait_ge(S("a_r"), i * 4 + (2 * pr + 2))
                    for k in range(2):
                        sg(dve.tensor_tensor_scan(a_g[:, k].rearrange("p j t -> p (j t)"), a_r[:].rearrange("p j t -> p (j t)"),
                                                  a_m[:, k].rearrange("p j t -> p (j t)"), 0.0, ALU.mult, ALU.add), "a_scanned")
                    dve.wait_ge(S("a_scanned"), i * 4 + (2 * pr + 2))
                    link(mul(a_t1[:], a_g[:], cos))
                    sg(mul(a_t2[:], a_g[:], sin), "a_P_used")
                    dve.wait_ge(S("a_P_used"), i * 2 + (pr + 3))
                    link(sub(a_m[:, 0], a_t1[:, 0], a_t2[:, 1]))
                    sg(add(a_m[:, 1], a_t1[:, 1], a_t2[:, 0]), "a_H")
                    dve.wait_ge(S("a_H"), i * 2 + (pr + 1))
                    tiles = bass.ds(i * 4 + 2 * pr, 2)
                    link(dve.tensor_copy(a_last[:, :, tiles, 0:1], a_m[:, :, :, SEQ - 1:SEQ]))
                    for k in range(2):
                        link(ts(a_last[:, k, tiles, 1:N_SEQ],
                                a_m[:, k, :, SEQ:T].rearrange("p j (b t) -> p j b t", t=NT)[:, :, :, NT - 1], 1.0, None, ALU.mult))
                dve.wait_ge(S("a_y_part"), i * 2 + 2)
                link(stt(a_y[:], a_ud[:], a_d[:, bass.ds(i, 1)], ps[:, 6, 0:T], ALU.mult, ALU.add))
                link(mul(a_gs[:], a_y[:], a_y[:]))
                link(ts(a_gs[:], a_gs[:], 0.044715, 1.0, ALU.mult, ALU.add))
                sg(mul(a_gs[:], a_gs[:], a_y[:]), "a_inner")
                dve.wait_ge(S("a_tanh"), i + 1)
                sg(stt(a_th, a_th, 1.0, a_y[:], ALU.add, ALU.mult), "a_z2")
                dve.wait_ge(S("a_z2"), i + 1)
                link(mul(zg[:, bass.ds(i, 1), :], a_th.unsqueeze(1), a_gate[:].unsqueeze(1)))
                dve.wait_ge(S("a_z_hi"), i + 1)
                sg(low(z_lo[:, bass.ds(i, 1), :], a_th.unsqueeze(1), 0.5, z_hi[:, bass.ds(i, 1), :]), "a_z_lo")
            ch.leave(WT)
            with dve.Fori(0, 2) as i:
                split("glu", i, 0, 4)
                for b in range(4):
                    dve.wait_ge(S("glu_th"), i * 4 + (b + 1))
                    sg(stt(a_y[:].unsqueeze(1), a_th.unsqueeze(1), 1.0, zg[:, bass.ds(i * 4 + b, 1), :], ALU.add, ALU.mult), "glu_out")
                    dve.wait_ge(S("glu_hi"), i * 4 + (b + 1))
                    dve.wait_ge(S("glu_out"), i * 4 + (b + 1))
                    br = bass.ds(i * 4 + b, 1)
                    sg(low(br_lo[:, br, :], a_y[:].unsqueeze(1), 0.125, br_hi[:, br, :]), "glu_lo")
                    dve.wait_ge(S("glu_lo"), i * 4 + (b + 1))
            merge("mA", 4)

            dve.wait_ge(S("o_hi_ready"), 1)
            sg(sub(h_lo[:], acc[:], h_hi[:].bitcast(F32)), "o_split")
            split("out", 0, 0, 4)
            sums = half_out[:].unsqueeze(1)
            link(dve.memset(half_out[:], 0.0))
            with dve.Fori(0, 7) as i:
                ch.enter(i, 2)
                split("out", i, 4, 4)
                for b in range(2):
                    wait_taken(dve, "out", i, b)
                    link(add(sums, sums, o_sq[:, bass.ds(i * 2 + b, 1), :]))
            ch.leave(7)
            wait_taken(dve, "out", 7, 0)
            link(add(sums, sums, o_sq[:, 14:15, :]))
            wait_taken(dve, "out", 7, 1)
            sg(add(sums, sums, o_sq[:, 15:16, :]), "res_ksum")
            dve.wait_ge(S("res_sd"), 1)
            link(dve.reciprocal(rstd[:], sd[:]))
            dve.wait_ge(S("res_landed"), 16)
            for half in range(2):
                ks = slice(half * KT // 2, (half + 1) * KT // 2)
                link(mul(acc[:, ks], acc[:, ks], rstd[:].unsqueeze(1).to_broadcast([P, KT // 2, T])))
                for k in range(ks.start, ks.stop):
                    ins = stt(acc[:, k], acc[:, k], norm_cols[:, 1, k:k + 1], x_res[:, k], ALU.mult, ALU.add)
                sg(ins, "y_ready")

        @block.tensor
        def _(pe):
            def mm(out, a, b, start=True, stop=True):
                return pe.matmul(out, a, b, start=start, stop=stop)

            def sg(ins, name):
                ins.then_inc(S(name) if isinstance(name, str) else name, 1)

            def project(stage, i, b, u0, n_units, x_hi, x_lo, n, bank=None, units=(0, 1)):
                if bank is None:
                    bank = b % 2
                    pe.wait_ge(bank_free[bank], earlier(stage, i, b))
                for u in units[:n_units]:
                    slot = (u0 + u) % SLOTS
                    pe.wait_ge(lo_ready, at(stage, i, u0 + u) + 1)
                    for k in range(UK):
                        kt = u * UK + k
                        first, last = kt == 0, kt == n_units * UK - 1
                        mm(ps[:, bank, 0:n], w_hi[:, slot, k], x_hi[:, kt], first, False)
                        mm(ps[:, bank, 0:n], w_lo[:, slot, k], x_hi[:, kt], False, False)
                        ins = mm(ps[:, bank, 0:n], w_hi[:, slot, k], x_lo[:, kt], False, last)
                    sg(ins, slots_freed)

            def merge(stage, m):
                def pair(i, half, ahead):
                    pe.wait_ge(merge_done, i * 4 + (16 * m + 2 * half))
                    for d in range(2):
                        project(stage, i, None, 4 + 6 * half + d, 1, br_hi, br_lo, T, bank=2 + d)
                    if ahead:
                        for d in range(2):
                            project(stage, i, 2 * half + 2 + d, 6 + 6 * half + 2 * d, 2, h_hi, h_lo, T)

                with pe.Fori(0, 3) as i:
                    pair(i, 0, True)
                    pair(i, 1, True)
                pair(3, 0, True)
                pair(3, 1, stage != "mA")

            def sum_channels(pre, n):
                pe.wait_ge(S(pre + "_ksum"), 1)
                sg(mm(ps[:, 2, 0:n], ones[:], half_out[:, 0:n]), pre + "_summed")

            pe.wait_ge(S("ones_ready"), 1)
            sum_channels("x", T)
            pe.wait_ge(S("x_split"), 1)
            for b in range(2):
                project("E", 0, b, 2 * b, 2, h_hi, h_lo, T)
            sum_channels("mem", N_MEM)
            pe.wait_ge(S("masks_ready"), 1)
            pe.wait_ge(S("mem_split"), 1)

            with pe.Fori(0, 4) as i:
                for b in (2, 3):
                    project("E", i, b, 2 * b, 2, m_hi, m_lo, N_MEM)
                pe.wait_ge(S("e_lo"), i)
                wait_taken(pe, "E", i, 3)
                for tt in range(2):
                    for dt in range(2):
                        ins = mm(ps[:, 3, tt * N_MEM:(tt + 1) * N_MEM], eq[:, dt, tt * P:(tt + 1) * P], kT[:, dt], dt == 0, dt == 1)
                sg(ins, "e_scores")
                pe.wait_ge(S("kc_landed"), i * 16 + 16)
                for mt in range(2):
                    for b in range(NB):
                        for dt in range(2):
                            ins = mm(ps[:, 4, mt * TS + b * NT:mt * TS + (b + 1) * NT], kc[:, dt, b, mt * P:(mt + 1) * P],
                                     eq[:, dt, SEQ + b * NT:SEQ + (b + 1) * NT], dt == 0, dt == 1)
                sg(ins, "e_scores")
                project("E", i, 4, 8, 2, m_hi, m_lo, N_MEM)
                pe.wait_ge(S("e_ssc"), i + 1)
                for mt in range(2):
                    ins = pe.transpose(ps[0:TS, 5, mt * P:(mt + 1) * P], ssc[:, mt], ident[:])
                sg(ins, "e_scores")
                project("E", i, 5, 10, 2, m_hi, m_lo, N_MEM)
                wait_taken(pe, "E", i, 5)
                for mt in range(2):
                    for ct in range(2):
                        at_ = mt * HD + ct * P
                        ins = pe.transpose(ps[:, 6, at_:at_ + P], vT[:, ct, mt * P:(mt + 1) * P], ident[:])
                sg(ins, "e_vt")
                for b in (6, 7):
                    project("E", i, b, 2 * b, 2, h_hi, h_lo, T)
                pe.wait_ge(S("e_prob"), i * 3 + 3)
                for mt in range(2):
                    for tt in range(2):
                        pe.transpose(ps[:, 2, mt * SEQ + tt * P:mt * SEQ + (tt + 1) * P], prob[:, tt, mt * P:(mt + 1) * P], ident[:])
                    ins = pe.transpose(ps[:, 4, mt * TS:(mt + 1) * TS], prob[0:TS, 2, mt * P:(mt + 1) * P], ident[0:TS, 0:TS])
                sg(ins, "e_pt")
                project("E", i, 8, 16, 2, h_hi, h_lo, T)
                pe.wait_ge(S("e_pT"), i * 2 + 2)
                pe.wait_ge(S("e_vm"), i + 1)
                pe.wait_ge(S("vc_landed"), i * 16 + 16)
                for ct in range(2):
                    out = ps[:, 6 + ct]
                    for mt in range(2):
                        mm(out[:, 0:SEQ], vm[:, mt, ct * P:(ct + 1) * P], pT[:, mt, 0:SEQ], mt == 0, mt == 1)
                    for b in range(NB):
                        for mt in range(2):
                            seq = slice(SEQ + b * NT, SEQ + (b + 1) * NT)
                            ins = mm(out[:, seq], vc[:, mt, b, ct * P:(ct + 1) * P], pT[:, mt, seq], mt == 0, mt == 1)
                sg(ins, "e_o")
                project("E", i, 9, 18, 2, h_hi, h_lo, T)
            pe.wait_ge(S("e_lo"), 4)
            merge("mE", 0)

            with pe.Fori(0, WT) as i:
                project("D", i, 2, 4, 2, h_hi, h_lo, T)
                pe.wait_ge(S("d_xc"), i + 1)
                pe.wait_ge(S("d_w_landed"), i * 16 + 16)
                pe.wait_ge(S("d_i"), i)
                mm(ps[:, 2, 0:T], d_w[:, 0], xc[:])
                sg(mm(ps[:, 3, 0:T], d_w[:, 1], xc[:]), "d_gates")
                project("D", i, 3, 6, 2, h_hi, h_lo, T)
            pe.wait_ge(S("d_lo"), WT)
            merge("mD", 1)

            def mix(stage, i, nv, values, rest):
                heads, v0 = heads_before(i, nv)

                def w(name, per=1, k=1):
                    pe.wait_ge(S("g_" + name), heads * per + k)

                def wv(name, k):
                    pe.wait_ge(S("g_" + name), v0 + k)

                for b in range(2, values + 1):
                    project(stage, i, b, 2 * b, 2, h_hi, h_lo, T)
                wait_taken(pe, stage, i, values)
                wv("out", 0)
                w("new", 1, 0)
                w("Sp", 1, 0)
                for v in range(nv):
                    for tt in range(2):
                        pe.transpose(ps[:, 2 + tt, v * P:(v + 1) * P], g_v[:, v, tt * P:(tt + 1) * P], ident[:])
                    ins = pe.transpose(ps[0:TS, 4, v * P:(v + 1) * P], g_v[:, v, SEQ:T], ident[:])
                sg(ins, "g_vt")
                for b in range(values + 1, rest + 1):
                    project(stage, i, b, 2 * b, 2, h_hi, h_lo, T)
                w("X")
                w("vT", 3, 3)
                lev = ps[:, 2:4].rearrange("p a (l t) -> p (a l) t", t=P)

                def pairs(tok):
                    for l in range(7):
                        mm(lev[:, l], g_X[:, l, tok], g_X[:, l, tok])
                    sg(mm(lev[:, DIAG], g_k[:, tok], g_q[:, tok]), "g_levels")

                pairs(slice(0, P))
                for n, (a, b) in enumerate(((g_X[:, 5], g_X[:, 5]), (g_X[:, 6], g_X[:, 6]), (g_k, g_q))):
                    ins = mm(ps[0:TS, 4, n * TS:(n + 1) * TS], a[:, SEQ:T], b[:, SEQ:T])
                sg(ins, "g_levels")
                mm(ps[:, 6, 0:P], g_X[:, CROSS, 0:P], g_X[:, CROSS, P:2 * P])
                for tt in range(2):
                    pe.transpose(ps[:, 5, tt * P:(tt + 1) * P], g_X[:, FINAL, tt * P:(tt + 1) * P], ident[:])
                sg(pe.transpose(ps[0:TS, 5, 2 * P:3 * P], g_X[:, FINAL, SEQ:T], ident[:]), "g_kt")
                project(stage, i, rest + 1, 2 * rest + 2, 2, h_hi, h_lo, T, units=(0,))
                w("att", 3, 1)
                pairs(slice(P, 2 * P))
                project(stage, i, rest + 1, 2 * rest + 2, 2, h_hi, h_lo, T, units=(1,))
                w("att", 3, 3)
                w("cross_out")
                pe.wait_ge(S("g_S0_landed"), heads * 16 + 16)
                for v in range(nv):
                    out, val = ps[:, 2 + v], lambda n: g_vT[:, n, v * P:(v + 1) * P]
                    mm(out[:, 0:2 * P], val(0), g_att[:, 0:2].rearrange("p a t -> p (a t)"), True, False)
                    mm(out[:, P:2 * P], val(1), g_att[:, 2], False, False)
                    mm(out[:, SEQ:T], val(2)[0:TS], g_atts[:], False, False)
                    for b in range(NB):
                        seq = slice(SEQ + b * NT, SEQ + (b + 1) * NT)
                        ins = mm(out[:, seq], g_S0[:, b, v * P:(v + 1) * P], g_X[:, CROSS, seq], False, b == NB - 1)
                sg(ins, "g_o")
                w("kT", 2, 2)
                mm(ps[:, 4, 0:nv * P], g_kT[:, 0], g_vT[:, 0, 0:nv * P], True, False)
                sg(mm(ps[:, 4, 0:nv * P], g_kT[:, 1], g_vT[:, 1, 0:nv * P], False, True), "g_Sp_raw")

                def updates(half):
                    wv("vm", half + 1)
                    if half:
                        w("half_new")
                    mm(ps[:, 5], g_kT[0:TS, 2], g_vm[:, 0:512])
                    sg(mm(ps[:, 6], g_kT[0:TS, 2], g_vm[:, 512:1024]), "g_up")

                updates(0)
                wv("sq", nv)
                for v in range(nv):
                    ins = mm(ps[:, 7, 0:T], ones[:], g_o2[:, v], v == 0, v == nv - 1)
                sg(ins, "g_ssq")
                if nv == 2:
                    updates(1)

            pe.wait_ge(S("g_params"), 48)
            for n, part in enumerate((h_hi, h_lo)):
                for k in range(KT):
                    ins = mm(ps[0:GLA_RANK, 2, 0:T], g_wr[:, k], part[:, k].bitcast(F32), n + k == 0, n == 1 and k == KT - 1)
            sg(ins, "c_rT_raw")
            pe.wait_ge(S("c_rT"), 1)
            with pe.Fori(0, 4) as i:
                pe.wait_ge(S("c_wu_landed"), i * 16 + 16)
                pe.wait_ge(S("g_out"), i * 2)
                sg(mm(ps[:, 7, 0:T], g_wu[:], g_r[:]), "c_z")
                mix("C", i, 2, 3, 6)
            pe.wait_ge(S("g_lo"), 8)
            merge("mC", 2)

            with pe.Fori(0, 8) as i:
                mix("B", i, 1, 2, 4)
            pe.wait_ge(S("g_lo"), 16)
            merge("mB", 3)

            with pe.Fori(0, WT) as i:
                wait_taken(pe, "A", i, 0)
                pe.wait_ge(S("a_B"), i * 2 + 2)
                pe.wait_ge(S("a_C"), i * 2 + 2)

                def inputs(pr):
                    pe.wait_ge(S("a_x_used"), i * 2 + pr)
                    for k in range(2):
                        for j in range(2):
                            lhsT = a_B[:, k, 2 * (2 * pr + j):2 * (2 * pr + j) + 2, :].rearrange("p g s -> p (g s)")
                            ins = mm(ps[:, 2 + 2 * k + j, 0:T], lhsT, a_ud[:])
                    sg(ins, "a_x")

                def outputs(pr):
                    pe.wait_ge(S("a_H"), i * 2 + (pr + 1))
                    for k in range(2):
                        for j in range(2):
                            ins = mm(ps[:, 6, 0:T], a_C[:, k, 2 * pr + j], a_m[:, k, j],
                                     pr + k + j == 0, pr + k + j == 3)
                    sg(ins, "a_y_part")

                inputs(0)
                project("A", i, 2, 4, 2, h_hi, h_lo, T)
                inputs(1)
                project("A", i, 3, 6, 2, h_hi, h_lo, T)
                outputs(0)
                outputs(1)
            pe.wait_ge(S("a_z_lo"), WT)
            with pe.Fori(0, 2) as i:
                for b in range(4):
                    pe.wait_ge(S("glu_th"), i * 4 + max(b - 1, 0))
                    project("glu", i, None, b, 1, z_hi, z_lo, T, bank=2 + b % 2)
            pe.wait_ge(S("glu_lo"), WT)
            merge("mA", 4)

            pe.wait_ge(S("o_split"), 1)
            with pe.Fori(0, 8) as i:
                for b in range(2):
                    project("out", i, b, 2 * b, 2, h_hi, h_lo, T)
            sum_channels("res", T)


SPLITS = (("a_x", W), ("a_g", W), ("b_q", W), ("b_f", W), ("b_i", W), ("b_g", W), ("c_q", W // 2), ("c_k", W // 2),
          ("c_v", W), ("c_r", GLA_RANK), ("c_g", W), ("d_x", W), ("d_g", W), ("e_q", W), ("e_g", W))


def blocks(w):
    rows, cols = w.shape
    return w.reshape(rows // (UK * P), UK, P, cols // P, P).transpose(3, 0, 2, 1, 4).reshape(cols // P, -1, P, UK * P)


def heads(n, *parts):
    return np.concatenate([p.reshape(n, -1, P, UK * P) for p in parts], axis=1).reshape(-1, P, UK * P)


def tiles(a):
    a = a.reshape(*a.shape[:-1], -1, P)
    return np.moveaxis(np.moveaxis(a, -1, 0), -1, 1)


def layout(x):
    x = {k: np.asarray(v) for k, v in x.items()}
    g = {k: v[0] for k, v in x.items() if k not in ("x_prompt", "x_sample", "mem_prompt")}
    at, win = 0, {}
    for name, width in SPLITS:
        win[name] = g["w_in"][:, at:at + width]
        at += width
    wb = {name: blocks(w) for name, w in win.items() if name != "c_r"}
    def merge(n):
        gates = blocks(g["w_merge"][:, n * D_MODEL:(n + 1) * D_MODEL]).reshape(KT // 2, 4, P, UK * P)
        branch = blocks(g["w_branch"][n]).reshape(KT // 2, 2, P, UK * P)
        rest = np.concatenate([branch[:-1], gates[1:]], axis=1).reshape(-1, P, UK * P)
        return gates[0], np.concatenate([rest, branch[-1]])

    first_gates, rest_of_merge = merge(0)
    stream = np.concatenate([
        heads(4, wb["e_q"], blocks(g["w_mem_k"]), blocks(g["w_mem_v"]), wb["e_g"]), *merge(4),
        heads(WT, wb["d_x"], wb["d_g"]), *merge(3),
        heads(4, wb["c_q"], wb["c_k"], wb["c_v"], wb["c_g"]), *merge(2),
        heads(8, wb["b_f"], wb["b_q"], wb["b_i"], wb["b_g"]), *merge(1),
        heads(WT, wb["a_x"], wb["a_g"]), first_gates, heads(WT, blocks(g["s5_w_glu"])), rest_of_merge,
        heads(KT, blocks(g["w_out"]))])
    tok = np.concatenate([x["x_prompt"][0], x["x_sample"].reshape(TS, D_MODEL)])

    def cache(a):
        return a.reshape(NB, N_MEM, 4, HD).transpose(2, 0, 1, 3)

    kc = cache(g["cache_mem_k"]).reshape(4, NB, N_MEM, 2, P).transpose(0, 4, 3, 1, 2)
    vc = cache(g["cache_mem_v"]).reshape(4, NB, 2, P, HD).transpose(0, 3, 2, 1, 4)
    states = lambda a: a.reshape(32, P, *a.shape[1:]).swapaxes(0, 1)
    flat = lambda a: a.reshape(-1, *a.shape[2:])
    rep = lambda a: np.repeat(a, 16, axis=0).reshape(WT, P, -1).swapaxes(0, 1)
    chan = lambda a: a.transpose(0, 2, 1).reshape(WT, P, 64).swapaxes(0, 1)
    out = {
        "w": stream,
        "mem": tiles(x["mem_prompt"][0]), "x": tiles(tok),
        "norms": np.stack([tiles(g[n]) for n in ("norm_pre", "norm_post", "mem_norm")], 1),
        "kc": kc, "vc": vc,
        "d_cols": np.stack([tiles(a) for a in (*g["conv_w"], g["conv_b"], g["lru_b_r"], g["lru_b_i"], g["lru_lam"])], 1),
        "d_cbuf": tiles(g["state_conv"]), "d_h0": tiles(g["state_rglru"]),
        "d_w": np.stack([g["lru_w_r"], g["lru_w_i"]], 2),
        "g_cols": np.concatenate([tiles(g["gla_norm"]), tiles(g["hg_norm"]), tiles(g["hg_norm"]), tiles(g["gla_b_up"])], 1),
        "lb": tiles(g["hg_lb_logits"]),
        "w_r": win["c_r"].reshape(KT, P, GLA_RANK).swapaxes(0, 1),
        "w_up": g["gla_w_up"].reshape(GLA_RANK, 4, P).swapaxes(0, 1),
        "gla": g["state_gla"].transpose(1, 2, 0, 3), "hgrn": g["state_hgrn"].transpose(1, 2, 0, 3),
        "a_state": np.stack([states(flat(g["s5_lam_re"])), states(flat(g["s5_lam_im"])),
                             states(np.repeat(g["s5_log_dt"], 64))], 1),
        "a_chan": np.stack([rep(g["s5_lam_re"]), rep(g["s5_lam_im"])], 1),
        "a_chan_dt": rep(g["s5_log_dt"][:, None])[:, :, 0],
        "a_br": chan(g["s5_b_re"]), "a_bi": chan(g["s5_b_im"]),
        "a_h0": np.stack([states(g[n].reshape(NB, -1).T) for n in ("state_s5_re", "state_s5_im")], 1),
        "a_d": tiles(g["s5_d"]),
        "a_c": np.stack([states(flat(g[n].transpose(0, 2, 1))) for n in ("s5_c_re", "s5_c_im")], 1),
    }
    return {k: np.ascontiguousarray(v) for k, v in out.items()}


OUTPUTS = {"out_y": (P, KT, T), "out_mem_k": (4, P, 2, N_MEM), "out_mem_v": (4, P, 2, N_MEM),
           "out_lru": (P, WT, N_SEQ), "out_conv": (P, WT, N_SEQ, 3),
           "out_gla_s": (4, P, NB, 256), "out_gla_p": (4, P, 256),
           "out_hg_s": (8, P, NB, P), "out_hg_p": (8, P, P), "out_s5": (P, 2, 32, N_SEQ)}


def kernel(**inputs):
    import concourse.bacc as bacc
    from concourse.bass_utils import run_bass_kernel_spmd

    nc = bacc.Bacc("TRN2", target_bir_lowering=False, num_devices=1)
    arrays = layout(inputs)
    t = {name: nc.dram_tensor(f"in_{name}", a.shape, F32, kind="ExternalInput").ap() for name, a in arrays.items()}
    t.update({name: nc.dram_tensor(name, shape, F32, kind="ExternalOutput").ap() for name, shape in OUTPUTS.items()})
    build(nc, t)
    r = run_bass_kernel_spmd(nc, [{f"in_{name}": a for name, a in arrays.items()}], core_ids=[0]).results[0]
    r = {name: np.asarray(r[name]) for name in OUTPUTS}

    y = r["out_y"].transpose(2, 1, 0).reshape(T, D_MODEL)
    mem = lambda a: a.transpose(3, 0, 2, 1).reshape(1, 1, N_MEM, 4, HD)
    lru = r["out_lru"].transpose(2, 1, 0).reshape(N_SEQ, W)
    conv = r["out_conv"].transpose(2, 3, 1, 0).reshape(N_SEQ, 3, W)
    s5 = r["out_s5"].transpose(1, 3, 2, 0).reshape(2, N_SEQ, 64, 64)
    gla_s, hg_s = (r[n].transpose(2, 0, 1, 3)[None] for n in ("out_gla_s", "out_hg_s"))
    gla_p, hg_p = r["out_gla_p"][None, None], r["out_hg_p"][None, None]
    result = (y[None, :SEQ], y[SEQ:].reshape(NB, NT, D_MODEL),
              s5[0, None, :1], s5[1, None, :1], hg_p, gla_p, lru[None, :1], conv[None, :1],
              mem(r["out_mem_k"]), mem(r["out_mem_v"]),
              s5[0, None, 1:], s5[1, None, 1:], hg_s, gla_s, lru[None, 1:], conv[None, 1:])
    return tuple(np.ascontiguousarray(a) for a in result)
```
